# Optimizing a Trainium2 kernel written in Bass

```python
import math
import jax, jax.numpy as jnp
from jax import lax
import numpy as np

D_MODEL = 1024
BATCH = 1
SEQ = 256
DEPTH = 2

GRID_W = 64
CTX_LEN = 256
ATTN_HEADS = 8
ATTN_KV_HEADS = 2
ATTN_HEAD_DIM = 64
WINDOW = 128
ATTN_BLOCK = 128
ROPE_THETA = 10000.0
GDN_HEADS = 4
GDN_HEAD_DIM = 128
GDN_W = GDN_HEADS * GDN_HEAD_DIM
GDN_CONV = 5
GDN_CHUNK = 64
POOL_SIZES = (2, 4, 8, 16)
POOL_GROUP = 128
POOL_WIDTH = POOL_GROUP * len(POOL_SIZES)
D_FF = 2816
N_MOD = 9
N_BRANCH = 3
EPS = 1e-6
IN_SIZES = (ATTN_HEADS * ATTN_HEAD_DIM, ATTN_KV_HEADS * ATTN_HEAD_DIM, ATTN_KV_HEADS * ATTN_HEAD_DIM,
            3 * GDN_W, GDN_W, 4 * GDN_HEADS, POOL_WIDTH, N_BRANCH * D_MODEL)
IN_WIDTH = sum(IN_SIZES)

kernel_name = 'hybrid_gated_parallel_diffusion_block'

def rms_norm(x, gain):
    x32 = x.astype(jnp.float32)
    y = x32 * lax.rsqrt(jnp.mean(x32 * x32, axis=-1, keepdims=True) + EPS)
    return (y * gain.astype(jnp.float32)).astype(x.dtype)

def modulate(h, shift, scale):
    return h * (1 + scale) + shift

def swiglu(h, w_in, w_out):
    gt, up = jnp.split(h @ w_in, 2, axis=-1)
    return (jax.nn.silu(gt) * up) @ w_out

def rope_axis(x, pos):
    half = x.shape[-1] // 2
    inv = ROPE_THETA ** (-jnp.arange(half, dtype=jnp.float32) / half)
    ang = pos.astype(jnp.float32)[:, None] * inv[None, :]
    cos = jnp.cos(ang)[:, None, :].astype(x.dtype)
    sin = jnp.sin(ang)[:, None, :].astype(x.dtype)
    x1, x2 = x[..., :half], x[..., half:]
    return jnp.concatenate([x1 * cos - x2 * sin, x1 * sin + x2 * cos], axis=-1)

def rope_2d(x, row, col):
    hd2 = x.shape[-1] // 2
    return jnp.concatenate([rope_axis(x[..., :hd2], row), rope_axis(x[..., hd2:], col)], axis=-1)

def window_attention(q, k, v, kc, vc, sink):
    B, L, Hkv, G, dh = q.shape
    NB = L // ATTN_BLOCK
    scale = dh ** -0.5
    qb = q.reshape(B, NB, ATTN_BLOCK, Hkv, G, dh)

    def band(t):
        tp = jnp.pad(t, ((0, 0), (ATTN_BLOCK, ATTN_BLOCK), (0, 0), (0, 0)))
        tp = tp.reshape(B, NB + 2, ATTN_BLOCK, Hkv, dh)
        return jnp.concatenate([tp[:, :-2], tp[:, 1:-1], tp[:, 2:]], axis=2)

    kw, vw = band(k), band(v)
    s_win = jnp.einsum('bnqhgd,bnkhd->bnhgqk', qb, kw, preferred_element_type=jnp.float32) * scale
    rel = jnp.arange(3 * ATTN_BLOCK)[None, :] - ATTN_BLOCK - jnp.arange(ATTN_BLOCK)[:, None]
    kpos = (jnp.arange(NB)[:, None] - 1) * ATTN_BLOCK + jnp.arange(3 * ATTN_BLOCK)[None, :]
    valid = (jnp.abs(rel) <= WINDOW)[None] & ((kpos >= 0) & (kpos < L))[:, None, :]
    s_win = jnp.where(valid[None, :, None, None], s_win, -jnp.inf)
    s_ctx = jnp.einsum('bnqhgd,bkhd->bnhgqk', qb, kc, preferred_element_type=jnp.float32) * scale
    sk = sink.astype(jnp.float32)[None, None, :, :, None]
    m = jnp.maximum(jnp.maximum(s_win.max(-1), s_ctx.max(-1)), sk)
    p_win = jnp.exp(s_win - m[..., None])
    p_ctx = jnp.exp(s_ctx - m[..., None])
    denom = p_win.sum(-1) + p_ctx.sum(-1) + jnp.exp(sk - m)
    o = (jnp.einsum('bnhgqk,bnkhd->bnqhgd', p_win.astype(vw.dtype), vw, preferred_element_type=jnp.float32)
         + jnp.einsum('bnhgqk,bkhd->bnqhgd', p_ctx.astype(vc.dtype), vc, preferred_element_type=jnp.float32))
    o = o / jnp.transpose(denom, (0, 1, 4, 2, 3))[..., None]
    return o.astype(q.dtype).reshape(B, L, Hkv * G * dh)

def context_attention(qc, kc, vc, sink):
    B, Lc, Hkv, G, dh = qc.shape
    s = jnp.einsum('bqhgd,bkhd->bhgqk', qc, kc, preferred_element_type=jnp.float32) * dh ** -0.5
    sk = sink.astype(jnp.float32)[None, :, :, None]
    m = jnp.maximum(s.max(-1), sk)
    p = jnp.exp(s - m[..., None])
    denom = p.sum(-1) + jnp.exp(sk - m)
    o = jnp.einsum('bhgqk,bkhd->bqhgd', p.astype(vc.dtype), vc, preferred_element_type=jnp.float32)
    o = o / jnp.transpose(denom, (0, 3, 1, 2))[..., None]
    return o.astype(qc.dtype).reshape(B, Lc, Hkv * G * dh)

def short_conv(x, w):
    K, C = w.shape
    pad = (K - 1) // 2
    y = lax.conv_general_dilated(x, w[:, None, :], window_strides=(1,), padding=[(pad, pad)],
                                 dimension_numbers=('NWC', 'WIO', 'NWC'), feature_group_count=C)
    return jax.nn.silu(y)

def l2norm(x):
    return x * lax.rsqrt(jnp.sum(x * x, axis=-1, keepdims=True) + EPS)

def gdn_chunk(q, k, v, g, beta, S0):
    B, L, H, dk = q.shape
    dv = v.shape[-1]
    out_dtype = v.dtype
    C = GDN_CHUNK
    N = L // C
    f32 = jnp.float32

    def chunks(t):
        t = t.astype(f32).reshape((B, N, C, H) + t.shape[3:])
        return jnp.moveaxis(t, 3, 1)

    q = chunks(l2norm(q.astype(f32)) * dk ** -0.5)
    k = chunks(l2norm(k.astype(f32)))
    v = chunks(v)
    g = chunks(g)
    beta = chunks(beta)
    gc = jnp.cumsum(g, axis=-1)
    diff = gc[..., :, None] - gc[..., None, :]
    strict = jnp.tril(jnp.ones((C, C), bool), -1)
    incl = jnp.tril(jnp.ones((C, C), bool))
    kk = jnp.einsum('bhnid,bhnjd->bhnij', k, k)
    a_mat = beta[..., :, None] * kk * jnp.exp(jnp.where(strict, diff, -jnp.inf))
    eye = jnp.eye(C, dtype=f32)
    t_mat = lax.linalg.triangular_solve(eye + a_mat, jnp.broadcast_to(eye, a_mat.shape),
                                        left_side=True, lower=True, unit_diagonal=True)
    u = t_mat @ (beta[..., None] * v)
    w = t_mat @ ((beta * jnp.exp(gc))[..., None] * k)
    qk = jnp.einsum('bhnid,bhnjd->bhnij', q, k) * jnp.exp(jnp.where(incl, diff, -jnp.inf))
    q_dec = q * jnp.exp(gc)[..., None]
    k_dec = k * jnp.exp(gc[..., -1:] - gc)[..., None]
    g_tot = jnp.exp(gc[..., -1])

    def step(S, inp):
        u_n, w_n, qd_n, kd_n, qk_n, gt_n = inp
        v_new = u_n - w_n @ S
        o_n = qd_n @ S + qk_n @ v_new
        S = S * gt_n[..., None, None] + jnp.swapaxes(kd_n, -1, -2) @ v_new
        return S, o_n

    xs = tuple(jnp.moveaxis(t, 2, 0) for t in (u, w, q_dec, k_dec, qk, g_tot))
    S, o = lax.scan(step, S0.astype(f32), xs)
    o = o.transpose(1, 0, 3, 2, 4).reshape(B, L, H, dv)
    return o.astype(out_dtype), S

def gdn_bidirectional(qkv, ab, conv_w, a_log, dt_bias, S0_f, S0_b):
    B, L, _ = qkv.shape
    qkv = short_conv(qkv, conv_w)
    q, k, v = [t.reshape(B, L, GDN_HEADS, GDN_HEAD_DIM) for t in jnp.split(qkv, 3, axis=-1)]
    a_f, a_b, b_f, b_b = jnp.split(ab.astype(jnp.float32), 4, axis=-1)
    f32 = jnp.float32
    g_f = -jnp.exp(a_log[0].astype(f32)) * jax.nn.softplus(a_f + dt_bias[0].astype(f32))
    g_b = -jnp.exp(a_log[1].astype(f32)) * jax.nn.softplus(a_b + dt_bias[1].astype(f32))
    beta_f = jax.nn.sigmoid(b_f)
    beta_b = jax.nn.sigmoid(b_b)
    flip = lambda t: jnp.flip(t, axis=1)
    o_f, S_f = gdn_chunk(q, k, v, g_f, beta_f, S0_f)
    o_b, S_b = gdn_chunk(flip(q), flip(k), flip(v), flip(g_b), flip(beta_b), S0_b)
    return o_f + flip(o_b), S_f, S_b

def gated_rms(o, z, gain):
    B, L, H, dv = o.shape
    o32 = o.astype(jnp.float32)
    o32 = o32 * lax.rsqrt(jnp.mean(o32 * o32, axis=-1, keepdims=True) + EPS) * gain.astype(jnp.float32)
    out = o32 * jax.nn.silu(z.astype(jnp.float32)).reshape(B, L, H, dv)
    return out.reshape(B, L, H * dv).astype(z.dtype)

def multiscale_pool(p, pool_w, pool_scale):
    B, L, W = p.shape
    p32 = p.astype(jnp.float32)
    cs = jnp.concatenate([jnp.zeros((B, 1, W), jnp.float32), jnp.cumsum(p32, axis=1)], axis=1)
    t = jnp.arange(L)
    outs = []
    for gi, win in enumerate(POOL_SIZES):
        lo = jnp.clip(t - win // 2, 0, L)
        hi = jnp.clip(t + win // 2, 0, L)
        csg = cs[..., gi * POOL_GROUP:(gi + 1) * POOL_GROUP]
        s = jnp.take(csg, hi, axis=1) - jnp.take(csg, lo, axis=1)
        cnt = (hi - lo).astype(jnp.float32)[None, :, None]
        outs.append(s / cnt - p32[..., gi * POOL_GROUP:(gi + 1) * POOL_GROUP])
    r = jnp.stack(outs, axis=2).astype(p.dtype)
    r = jnp.einsum('blgc,gcd->blgd', r, pool_w)
    return r.reshape(B, L, POOL_WIDTH) * pool_scale

def merge_branches(attn_o, gdn_o, pool_o, gate_logits, w_b_attn, w_b_gdn, w_b_pool, w_out):
    gates = jax.nn.sigmoid(gate_logits.reshape(gate_logits.shape[:-1] + (N_BRANCH, D_MODEL)))
    merged = (gates[..., 0, :] * (attn_o @ w_b_attn)
              + gates[..., 1, :] * (gdn_o @ w_b_gdn)
              + gates[..., 2, :] * (pool_o @ w_b_pool))
    return merged @ w_out

def hybrid_mixer(h, hc, row, col, w_in, attn_sink, conv_w, a_log, dt_bias, gdn_norm, pool_w, pool_scale,
                 w_b_attn, w_b_gdn, w_b_pool, w_out, need_ctx):
    B, L, _ = h.shape
    Lc = hc.shape[1]
    G = ATTN_HEADS // ATTN_KV_HEADS
    split = np.cumsum(IN_SIZES)[:-1].tolist()
    q, k, v, qkv, zg, ab, pin, gl = jnp.split(h @ w_in, split, axis=-1)
    qc, kc, vc, qkv_c, zg_c, ab_c, pin_c, gl_c = jnp.split(hc @ w_in, split, axis=-1)
    heads = lambda t, n: t.reshape(t.shape[:2] + (n, ATTN_HEAD_DIM))
    q = rope_2d(heads(q, ATTN_HEADS), row, col).reshape(B, L, ATTN_KV_HEADS, G, ATTN_HEAD_DIM)
    k = rope_2d(heads(k, ATTN_KV_HEADS), row, col)
    v = heads(v, ATTN_KV_HEADS)
    kc = heads(kc, ATTN_KV_HEADS)
    vc = heads(vc, ATTN_KV_HEADS)
    sink = attn_sink.reshape(ATTN_KV_HEADS, G)
    attn_o = window_attention(q, k, v, kc, vc, sink)
    S0 = jnp.zeros((B, GDN_HEADS, GDN_HEAD_DIM, GDN_HEAD_DIM), jnp.float32)
    oc_gdn, S_f, S_b = gdn_bidirectional(qkv_c, ab_c, conv_w, a_log, dt_bias, S0, S0)
    o_gdn, _, _ = gdn_bidirectional(qkv, ab, conv_w, a_log, dt_bias, S_f, S_b)
    gdn_o = gated_rms(o_gdn, zg, gdn_norm)
    pool_o = multiscale_pool(pin, pool_w, pool_scale)
    y = merge_branches(attn_o, gdn_o, pool_o, gl, w_b_attn, w_b_gdn, w_b_pool, w_out)
    if not need_ctx:
        return y, None
    attn_c = context_attention(qc.reshape(B, Lc, ATTN_KV_HEADS, G, ATTN_HEAD_DIM), kc, vc, sink)
    gdn_c = gated_rms(oc_gdn, zg_c, gdn_norm)
    pool_c = multiscale_pool(pin_c, pool_w, pool_scale)
    yc = merge_branches(attn_c, gdn_c, pool_c, gl_c, w_b_attn, w_b_gdn, w_b_pool, w_out)
    return y, yc

def setup_inputs(seed: int = 0) -> dict:
    key = jax.random.key(seed)
    ks = jax.random.split(key, 32)
    f32 = jnp.float32

    def nrm(i, shape, fan_in, gain=1.0):
        return jax.random.normal(ks[i], shape, f32) * (gain * fan_in ** -0.5)

    def gain_vec(i, shape):
        return 1.0 + 0.02 * jax.random.normal(ks[i], shape, f32)

    Dp = DEPTH
    dt = jnp.exp(jax.random.uniform(ks[14], (Dp, 2, GDN_HEADS), f32, math.log(1e-3), math.log(1e-1)))
    return {
        'x': jax.random.normal(ks[0], (BATCH, SEQ, D_MODEL), f32),
        'c': jax.random.normal(ks[1], (BATCH, D_MODEL), f32),
        'ctx': jax.random.normal(ks[2], (BATCH, CTX_LEN, D_MODEL), f32),
        'c_ctx': jax.random.normal(ks[3], (D_MODEL,), f32),
        'w_ada': nrm(4, (Dp, D_MODEL, N_MOD * D_MODEL), D_MODEL, 0.5),
        'b_ada': 0.02 * jax.random.normal(ks[5], (Dp, N_MOD * D_MODEL), f32),
        'norm_ffn1': gain_vec(6, (Dp, D_MODEL)),
        'w_ffn1_in': nrm(7, (Dp, D_MODEL, 2 * D_FF), D_MODEL),
        'w_ffn1_out': nrm(8, (Dp, D_FF, D_MODEL), D_FF),
        'norm_mix': gain_vec(9, (Dp, D_MODEL)),
        'w_in': nrm(10, (Dp, D_MODEL, IN_WIDTH), D_MODEL),
        'attn_sink': 0.5 * jax.random.normal(ks[11], (Dp, ATTN_HEADS), f32),
        'gdn_conv': nrm(12, (Dp, GDN_CONV, 3 * GDN_W), GDN_CONV),
        'gdn_a_log': jnp.log(jax.random.uniform(ks[13], (Dp, 2, GDN_HEADS), f32, 1.0, 16.0)),
        'gdn_dt_bias': dt + jnp.log(-jnp.expm1(-dt)),
        'gdn_norm': gain_vec(15, (Dp, GDN_HEAD_DIM)),
        'pool_w': nrm(16, (Dp, len(POOL_SIZES), POOL_GROUP, POOL_GROUP), POOL_GROUP),
        'pool_scale': 1.0 + 0.1 * jax.random.normal(ks[17], (Dp, POOL_WIDTH), f32),
        'w_branch_attn': nrm(18, (Dp, ATTN_HEADS * ATTN_HEAD_DIM, D_MODEL), ATTN_HEADS * ATTN_HEAD_DIM),
        'w_branch_gdn': nrm(19, (Dp, GDN_W, D_MODEL), GDN_W),
        'w_branch_pool': nrm(20, (Dp, POOL_WIDTH, D_MODEL), POOL_WIDTH),
        'w_out': nrm(21, (Dp, D_MODEL, D_MODEL), D_MODEL),
        'norm_ffn2': gain_vec(22, (Dp, D_MODEL)),
        'w_ffn2_in': nrm(23, (Dp, D_MODEL, 2 * D_FF), D_MODEL),
        'w_ffn2_out': nrm(24, (Dp, D_FF, D_MODEL), D_FF),
        'final_norm': gain_vec(25, (D_MODEL,)),
    }

def reference(x, c, ctx, c_ctx, w_ada, b_ada, norm_ffn1, w_ffn1_in, w_ffn1_out, norm_mix, w_in, attn_sink,
              gdn_conv, gdn_a_log, gdn_dt_bias, gdn_norm, pool_w, pool_scale, w_branch_attn, w_branch_gdn,
              w_branch_pool, w_out, norm_ffn2, w_ffn2_in, w_ffn2_out, final_norm):
    B, L, D = x.shape
    ROWS = L // GRID_W
    row = jnp.broadcast_to(jnp.arange(ROWS, dtype=jnp.int32)[:, None], (ROWS, GRID_W)).reshape(-1)
    col = jnp.broadcast_to(jnp.arange(GRID_W, dtype=jnp.int32)[None, :], (ROWS, GRID_W)).reshape(-1)
    sc = jax.nn.silu(c)
    scc = jax.nn.silu(c_ctx)
    xc = ctx
    for l in range(DEPTH):
        last = l == DEPTH - 1
        mod = (sc @ w_ada[l] + b_ada[l]).reshape(B, 1, N_MOD, D)
        modc = (scc @ w_ada[l] + b_ada[l]).reshape(N_MOD, D)
        m = [mod[:, :, i] for i in range(N_MOD)]
        mc = [modc[i] for i in range(N_MOD)]
        x = x + 0.5 * m[2] * swiglu(modulate(rms_norm(x, norm_ffn1[l]), m[0], m[1]), w_ffn1_in[l], w_ffn1_out[l])
        xc = xc + 0.5 * mc[2] * swiglu(modulate(rms_norm(xc, norm_ffn1[l]), mc[0], mc[1]), w_ffn1_in[l], w_ffn1_out[l])
        h = modulate(rms_norm(x, norm_mix[l]), m[3], m[4])
        hc = modulate(rms_norm(xc, norm_mix[l]), mc[3], mc[4])
        y, yc = hybrid_mixer(h, hc, row, col, w_in[l], attn_sink[l], gdn_conv[l], gdn_a_log[l], gdn_dt_bias[l],
                             gdn_norm[l], pool_w[l], pool_scale[l], w_branch_attn[l], w_branch_gdn[l],
                             w_branch_pool[l], w_out[l], not last)
        x = x + m[5] * y
        x = x + 0.5 * m[8] * swiglu(modulate(rms_norm(x, norm_ffn2[l]), m[6], m[7]), w_ffn2_in[l], w_ffn2_out[l])
        if not last:
            xc = xc + mc[5] * yc
            xc = xc + 0.5 * mc[8] * swiglu(modulate(rms_norm(xc, norm_ffn2[l]), mc[6], mc[7]), w_ffn2_in[l], w_ffn2_out[l])
    return rms_norm(x, final_norm)


_drawn_inputs = setup_inputs


def setup_inputs(seed=0):
    import zlib

    import numpy as np

    out = dict(_drawn_inputs(seed))
    spreads = {}
    factors = {'norm_ffn1': 8.0,
     'norm_mix': 8.0,
     'attn_sink': 8.0,
     'gdn_norm': 8.0,
     'norm_ffn2': 8.0,
     'final_norm': 2.803}
    for name, (base, spread) in spreads.items():
        noise = np.random.default_rng([zlib.crc32(name.encode()), seed]).standard_normal(out[name].shape)
        drawn = base * np.exp(spread * noise) if base else spread * noise
        out[name] = __import__('jax').numpy.asarray(drawn.astype(out[name].dtype))
    for name, factor in factors.items():
        out[name] = (out[name] * factor).astype(out[name].dtype)
    return out
```

```python
from contextlib import ExitStack, contextmanager
import math

import numpy as np
import concourse.bass as bass
from concourse import mybir

F32 = mybir.dt.float32
F32R = mybir.dt.float32r
ACT = mybir.ActivationFunctionType
ALU = mybir.AluOpType
AX = mybir.AxisListType

P = 128
D = 1024
KD = D // P
SEG = 256
TOK = 2 * SEG
LAT = SEG
DEPTH = 2
D_FF = 2816
HID_TILES = D_FF // P
CHUNKS = (8, 8, 6)
HEADS, KV_HEADS, DH = 8, 2, 64
WINDOW = 128
GH, GD = 4, 128
CONV = 5
PAD = CONV // 2
POOL_SIZES = (2, 4, 8, 16)
EPS = 1e-6
NEG = -1e30
LEVELS = 7
W_Q, W_K, W_V, W_QKV, W_ZG, W_AB, W_PIN, W_GL = 0, 512, 640, 768, 2304, 2816, 2832, 3344
MOD = 9 * KD
C_ID, C_ONE, C_TRI, C_NEG = 0, 128, 256, 512
C_LEV = 768
C_ROT = C_LEV + 2 * LEVELS * P
C_KD = C_ROT + P
C_COS = C_KD + 4 * P
C_SIN = C_COS + SEG
C_MASK = C_SIN + SEG
C_EDGE = C_MASK + 2 * TOK
C_END = C_EDGE + 4 * 2 * 8
V_N1, V_NM, V_N2, V_PS, V_GN, V_FIN, V_END = 0, 16, 32, 48, 56, 58, 66

PER_TRIP = {
    'act:att0': {'sc_ready': 16, 'act2': 8, 'act3': 8},
    'act:att256': {'sc_ready': 8, 'act2': 4, 'act3': 4},
    'act:ffn_in6False256': {'raw_in3': 1, 'block': 4, 'tile': 4, 'raw_in0': 1, 'hprod_ready': 2, 'raw_in1': 1, 'raw_in2': 1},
    'act:ffn_in6True0': {'raw_in0': 1, 'block': 4, 'tile': 4, 'raw_in1': 1, 'hprod_ready': 2, 'raw_in2': 1, 'raw_in3': 1},
    'act:ffn_in8False256': {'raw_in3': 1, 'block': 4, 'tile': 4, 'raw_in0': 1, 'hprod_ready': 2, 'raw_in1': 1, 'raw_in2': 1},
    'act:ffn_in8True0': {'raw_in0': 1, 'block': 4, 'tile': 4, 'raw_in1': 1, 'hprod_ready': 2, 'raw_in2': 1, 'raw_in3': 1},
    'act:ffn_out6True0': {'raw_in0': 1, 'block': 4, 'tile': 4, 'raw_in1': 1, 'raw_in2': 1, 'raw_in3': 1},
    'act:ffn_out8False256': {'raw_in3': 1, 'block': 4, 'tile': 4, 'raw_in0': 1, 'raw_in1': 1, 'raw_in2': 1},
    'act:ffn_out8True0': {'raw_in0': 1, 'block': 4, 'tile': 4, 'raw_in1': 1, 'raw_in2': 1, 'raw_in3': 1},
    'act:gdn': {'act0': 16, 'act3': 16, 'act_go': 4},
    'act:merge0': {'raw_in0': 1, 'block': 4, 'tile': 4, 'merged_ready': 2, 'raw_in1': 1, 'raw_in2': 1, 'raw_in3': 1},
    'act:merge256': {'raw_in3': 1, 'block': 4, 'tile': 4, 'merged_ready': 2, 'raw_in0': 1, 'raw_in1': 1, 'raw_in2': 1},
    'act:qknorm': {'sq_used': 2, 'act4': 1, 'act5': 1},
    'act:qkv0': {'raw_in0': 1, 'block': 4, 'tile': 4, 'pad_used': 4, 'raw_in1': 1, 'raw_in2': 1, 'raw_in3': 1},
    'act:qkv256': {'raw_in3': 1, 'block': 4, 'tile': 4, 'pad_used': 4, 'raw_in0': 1, 'raw_in1': 1, 'raw_in2': 1},
    'act:wout0': {'raw_in0': 1, 'block': 4, 'tile': 4, 'raw_in1': 1, 'raw_in2': 1, 'raw_in3': 1},
    'act:wout256': {'raw_in3': 1, 'block': 4, 'tile': 4, 'raw_in0': 1, 'raw_in1': 1, 'raw_in2': 1},
    'dve:ada': {'ada_done': 2},
    'dve:att0': {'dve4': 2, 'dve0': 8, 'dve1': 8, 'exp_ready': 16, 'dve5': 8, 'dve6': 8},
    'dve:att256': {'dve4': 2, 'dve0': 4, 'dve1': 4, 'exp_ready': 8, 'dve5': 4, 'dve6': 4},
    'dve:ffn_in6False256': {'hi_done': 4, 'block': 4, 'tile': 4, 'sil_ready': 2, 'hidhi_ready': 2},
    'dve:ffn_in6True0': {'hi_done': 4, 'block': 4, 'tile': 4, 'ada_done': 2, 'sil_ready': 2, 'hidhi_ready': 2},
    'dve:ffn_in8False256': {'hi_done': 4, 'block': 4, 'tile': 4, 'sil_ready': 2, 'hidhi_ready': 2},
    'dve:ffn_in8True0': {'hi_done': 4, 'block': 4, 'tile': 4, 'ada_done': 2, 'sil_ready': 2, 'hidhi_ready': 2},
    'dve:ffn_out6True0': {'hi_done': 4, 'block': 4, 'tile': 4, 'ada_done': 2},
    'dve:ffn_out8False256': {'hi_done': 4, 'block': 4, 'tile': 4},
    'dve:ffn_out8True0': {'hi_done': 4, 'block': 4, 'tile': 4, 'ada_done': 2},
    'dve:gdn': {'staged': 4, 'dve1': 18, 'dve4': 18, 'e_ready': 6, 'dve2': 16, 'dve0': 4, 'dve5': 16, 'dve3': 4},
    'dve:merge0False256': {'hi_done': 4, 'block': 4, 'tile': 4, 'sig_ready': 2},
    'dve:merge0True0': {'hi_done': 4, 'block': 4, 'tile': 4, 'ada_done': 2, 'sig_ready': 2},
    'dve:merge1False0': {'hi_done': 4, 'block': 4, 'tile': 4, 'sig_ready': 2},
    'dve:merge1False256': {'hi_done': 4, 'block': 4, 'tile': 4, 'sig_ready': 2},
    'dve:merge2False0': {'hi_done': 4, 'block': 4, 'tile': 4, 'sig_ready': 2},
    'dve:merge2False256': {'hi_done': 4, 'block': 4, 'tile': 4, 'sig_ready': 2},
    'dve:qknorm': {'rstd_ready': 2},
    'dve:qkv0True': {'hi_done': 4, 'block': 4, 'tile': 4, 'ada_done': 2, 'pad_ready': 4},
    'dve:qkv256False': {'hi_done': 4, 'block': 4, 'tile': 4, 'pad_ready': 4},
    'dve:woutFalse256': {'hi_done': 4, 'block': 4, 'tile': 4},
    'dve:woutTrue0': {'hi_done': 4, 'block': 4, 'tile': 4, 'ada_done': 2},
    'pe:ada': {'free7': 1, 'ada_in0': 1, 'ada_in1': 1},
    'pe:att0': {'free4': 2, 'qs_ready': 2, 'free0': 8, 'free1': 8, 'p_ready': 16, 'free2': 8, 'free3': 8, 'pT_ready': 16, 'free5': 8, 'free6': 8},
    'pe:att256': {'free4': 2, 'qs_ready': 2, 'free0': 4, 'free1': 4, 'p_ready': 8, 'free2': 4, 'free3': 4, 'pT_ready': 8, 'free5': 4, 'free6': 4},
    'pe:ffn_in6False': {'lo_done': 4, 'free2': 1, 'block': 4, 'free3': 1, 'free0': 1, 'free1': 1},
    'pe:ffn_in6True': {'free7': 1, 'ada_in0': 1, 'ada_in1': 1, 'lo_done': 4, 'free3': 1, 'block': 4, 'free0': 1, 'free1': 1, 'free2': 1},
    'pe:ffn_in8False': {'lo_done': 4, 'free2': 1, 'block': 4, 'free3': 1, 'free0': 1, 'free1': 1},
    'pe:ffn_in8True': {'free7': 1, 'ada_in0': 1, 'ada_in1': 1, 'lo_done': 4, 'free3': 1, 'block': 4, 'free0': 1, 'free1': 1, 'free2': 1},
    'pe:ffn_out6False': {'lo_done': 4, 'free2': 1, 'block': 4, 'free3': 1, 'free0': 1, 'free1': 1},
    'pe:ffn_out6True': {'free7': 1, 'ada_in0': 1, 'ada_in1': 1, 'lo_done': 4, 'free3': 1, 'block': 4, 'free0': 1, 'free1': 1, 'free2': 1},
    'pe:ffn_out8False': {'lo_done': 4, 'free2': 1, 'block': 4, 'free3': 1, 'free0': 1, 'free1': 1},
    'pe:ffn_out8True': {'free7': 1, 'ada_in0': 1, 'ada_in1': 1, 'lo_done': 4, 'free3': 1, 'block': 4, 'free0': 1, 'free1': 1, 'free2': 1},
    'pe:gdn': {'staged': 4, 'free0': 20, 'free3': 20, 'pe_go': 44, 'free1': 18, 'free4': 18, 'free2': 16, 'free5': 16, 'p_copied': 24},
    'pe:mergeFalse': {'lo_done': 4, 'free2': 1, 'block': 4, 'free3': 1, 'free0': 1, 'free1': 1},
    'pe:mergeTrue': {'free7': 1, 'ada_in0': 1, 'ada_in1': 1, 'lo_done': 4, 'free3': 1, 'block': 4, 'free0': 1, 'free1': 1, 'free2': 1},
    'pe:qknorm': {'sq_ready': 2, 'free4': 1, 'free5': 1},
    'pe:qkvFalse': {'lo_done': 4, 'free2': 1, 'block': 4, 'free3': 1, 'free0': 1, 'free1': 1},
    'pe:qkvTrue': {'free7': 1, 'ada_in0': 1, 'ada_in1': 1, 'lo_done': 4, 'free3': 1, 'block': 4, 'free0': 1, 'free1': 1, 'free2': 1},
    'pe:woutFalse': {'lo_done': 4, 'free2': 1, 'block': 4, 'free3': 1, 'free0': 1, 'free1': 1},
    'pe:woutTrue': {'free7': 1, 'ada_in0': 1, 'ada_in1': 1, 'lo_done': 4, 'free3': 1, 'block': 4, 'free0': 1, 'free1': 1, 'free2': 1},
    'pool:gdn': {'stage_free': 2},
    'sp:ada': {'ada_done': 2},
    'sp:ffn_in6False': {'lo_done': 4, 'block': 4},
    'sp:ffn_in6True': {'ada_done': 2, 'lo_done': 4, 'block': 4},
    'sp:ffn_in8False': {'lo_done': 4, 'block': 4},
    'sp:ffn_in8True': {'ada_done': 2, 'lo_done': 4, 'block': 4},
    'sp:ffn_out6False': {'lo_done': 4, 'block': 4},
    'sp:ffn_out6True': {'ada_done': 2, 'lo_done': 4, 'block': 4},
    'sp:ffn_out8False': {'lo_done': 4, 'block': 4},
    'sp:ffn_out8True': {'ada_done': 2, 'lo_done': 4, 'block': 4},
    'sp:mergeFalse': {'lo_done': 4, 'block': 4},
    'sp:mergeTrue': {'ada_done': 2, 'lo_done': 4, 'block': 4},
    'sp:qkvFalse': {'lo_done': 4, 'block': 4},
    'sp:qkvTrue': {'ada_done': 2, 'lo_done': 4, 'block': 4},
    'sp:woutFalse': {'lo_done': 4, 'block': 4},
    'sp:woutTrue': {'ada_done': 2, 'lo_done': 4, 'block': 4},
}


class Counts:

    def __init__(self, eng, sems, who, start, learned):
        self.e, self.sems, self.who, self.learned = eng, sems, who, learned
        self.base = dict(start)
        self.body, self.it, self.per = {}, None, {}

    def advance(self, name, k=1):
        if self.it is None:
            self.base[name] = self.base.get(name, 0) + k
        else:
            self.body[name] = self.body.get(name, 0) + k

    def static(self, name):
        return self.base.get(name, 0) + self.body.get(name, 0)

    def value(self, name, scale=1, plus=0):
        v = (self.static(name) + plus) * scale
        if self.it is not None and self.per.get(name, 0):
            v = self.it * (self.per[name] * scale) + v
        return v

    def next(self, name):
        self.advance(name)
        return self.value(name, 16 if name.startswith(("raw_in", "ada_in", "dma_")) else 1)

    @contextmanager
    def loop(self, name, trips):
        key = f"{self.who}:{name}"
        with self.e.Fori(0, trips) as it:
            self.it, self.per, self.body = it, PER_TRIP.get(key, {}), {}
            yield it
        if self.body != self.per:
            self.learned[key] = dict(self.body)
        for k, v in self.body.items():
            self.base[k] = self.base.get(k, 0) + v * trips
        self.body, self.it, self.per = {}, None, {}


def build(nc, a, out, learned):
    es = ExitStack()
    sems = {}

    def sb(name, shape, dt=F32, stack=es):
        return stack.enter_context(nc.sbuf_tensor(name, shape, dt))

    with es:
        xT = sb("xT", [P, KD, TOK])
        h_hi = sb("h_hi", [P, KD, TOK], F32R)
        h_lo = sb("h_lo", [P, KD, TOK], F32R)
        raw = sb("raw", [P, 4, 1024])
        w_hi = sb("w_hi", [P, 2, 1024], F32R)
        w_lo = sb("w_lo", [P, 2, 1024], F32R)
        ada_w = sb("ada_w", [P, 2, 1024])
        mod = sb("mod", [P, DEPTH * MOD, 2])
        bada = sb("bada", [P, DEPTH * MOD])
        con = sb("con", [P, C_END])
        vec = sb("vec", [P, V_END])
        convw = sb("convw", [P, DEPTH, CONV, 12])
        cT = sb("cT", [P, 2, KD])
        sink = sb("sink", [P, DEPTH, HEADS])
        alog = sb("alog", [P, DEPTH, 2, GH])
        dtb = sb("dtb", [P, DEPTH, 2, GH])
        bias = sb("bias", [P, 4])
        sq = sb("sq", [P, 2, TOK])
        acc = sb("acc", [P, TOK])
        rstd = sb("rstd", [P, 2, TOK])
        hx = sb("hx", [P, 2, TOK])
        am = sb("am", [P, KD, 2])
        gate = sb("gate", [P, KD, 2])
        gates = sb("gates", [P, 2, 4, GH])
        beta = sb("beta", [P, 2, 4, GH])
        gcn = sb("gcn", [P, 2, 4, GH])
        negeg = sb("negeg", [P, 2, 4, GH])
        gtot = sb("gtot", [P, 2, 4, GH])
        dec = sb("dec", [P, 2, 4, GH])
        gtmp = sb("gtmp", [P, 3, 2, 4, GH])
        stat = sb("stat", [P, 4, 6])
        ps = es.enter_context(nc.psum_tensor("ps", [P, 8, 512], F32))

        with ExitStack() as m:
            attnT = sb("attnT", [P, 4, TOK], F32, m)
            gdnT = sb("gdnT", [P, GH, TOK], F32, m)
            with ExitStack() as m2:
                qkvT = sb("qkvT", [P, 12, TOK], F32, m2)
                with ExitStack() as m3:
                    G = sb("G", [P, 2, 9, 4, P], F32, m3)
                    state = sb("state", [P, 2, GH, P], F32, m3)
                with ExitStack() as m3:
                    pad = sb("pad", [P, 2, 2, SEG + 2 * PAD], F32, m3)
                    kv = sb("kv", [P, 2, TOK], F32, m3)
                    kd = sb("kd", [P, KV_HEADS, TOK], F32, m3)
                    vnat = sb("vnat", [P, 4, P], F32, m3)
                    qs = sb("qs", [P, 2, TOK], F32, m3)
                    sc = sb("sc", [P, 3, TOK], F32, m3)
                    pT = sb("pT", [P, 2, 4, P], F32, m3)
                    rtmp = sb("rtmp", [P, 2, SEG], F32, m3)
            with ExitStack() as m2:
                poolT = sb("poolT", [P, 4, TOK], F32, m2)
                br_hi = sb("br_hi", [P, 4, TOK], F32R, m2)
                br_lo = sb("br_lo", [P, 4, TOK], F32R, m2)
                merged = sb("merged", [P, KD, TOK], F32, m2)
                sig = sb("sig", [P, 2, TOK], F32, m2)
                ppad = sb("ppad", [P, 2, 2, SEG + 16], F32, m2)
                pool_s = sb("pool_s", [P, 2, 2, SEG + 16], F32, m2)
                pw = sb("pw", [P, 4, P], F32, m2)
        with ExitStack() as m:
            hid_hi = sb("hid_hi", [P, 8, TOK], F32R, m)
            hid_lo = sb("hid_lo", [P, 8, TOK], F32R, m)
            sil = sb("sil", [P, 2, TOK], F32, m)
            hprod = sb("hprod", [P, 2, TOK], F32, m)
        with ExitStack() as m:
            rows = sb("rows", [P, 4, D], F32, m)
            vrows = sb("vrows", [P, 6, P], F32, m)

        KTS, QS, VN, EE, NT, TT, UU, PP, NM = range(9)

        names = (["hi_done", "lo_done", "tile_done", "ada_done", "dma_setup", "dma_out", "dma_pw"]
                 + [f"raw_in{i}" for i in range(4)] + [f"ada_in{i}" for i in range(2)]
                 + [f"free{b}" for b in range(8)] + [f"act{b}" for b in range(8)] + [f"dve{b}" for b in range(8)]
                 + ["x_ready", "sq_ready", "sq_used", "ssq_ready", "rstd_ready", "hx_ready", "hhi_ready",
                    "h_ready", "sil_ready", "hprod_ready", "hidhi_ready", "hid_ready", "c_ready", "zero_ready",
                    "kv_ready", "kd_ready", "qraw_ready", "qs_ready", "pad_ready", "pad_used", "conv_ready",
                    "silu_ready", "qkn_ready", "sc_ready", "exp_ready", "p_ready", "pT_ready", "act_go", "pe_go", "p_copied", "e_ready", "gdn_over", "sqn_ready",
                    "stage_free", "staged", "ab_ready", "abexp_ready", "g_ready", "gcx_ready",
                    "o_ready", "osq_ready", "z_ready", "br_ready", "brhi_ready", "brlo_ready", "sig_ready", "pin_ready",
                    "pool_ready", "merged_ready", "mhi_ready", "mlo_ready", "fin_ready", "o_out", "unused"])
        for n in names:
            sems[n] = es.enter_context(nc.semaphore(n))
        CREDIT = {"lo_done": 4, "tile_done": 1, "ada_done": 2, "sq_used": 2, }

        def counts(eng, who, credited):
            return Counts(eng, sems, who, {n: CREDIT[n] for n in credited}, learned)

        ident = con[:, C_ID:C_ID + P]
        ones = con[:, C_ONE:C_ONE + P]

        def tri(d):
            return con[:, C_TRI + d * P:C_TRI + (d + 1) * P]

        def negm(d):
            return con[:, C_NEG + d * P:C_NEG + (d + 1) * P]

        def lev(d, s):
            o = C_LEV + (d * LEVELS + s) * P
            return con[:, o:o + P]

        def heads(ap):
            return ap.rearrange("p (a b) -> p a b", a=1).to_broadcast([P, GH, P])

        def bank4(b):
            return ps[:, b, :].rearrange("p (h c) -> p h c", h=4)

        sides = {0: ((0, SEG, 0), (SEG, TOK, 1)), LAT: ((SEG, TOK, 1),)}

        def sp_block(c, src, k0, nk, col, width=P):
            s = c.static("block") % 4
            c.e.wait_ge(sems["lo_done"], c.next("lo_done"))
            c.e.sem_inc(sems["unused"], 1)
            dst = raw[:, s, 0:nk * width].rearrange("p (k c) -> p k c", k=nk)
            c.e.dma_start(dst, src[k0 * P:(k0 + nk) * P, bass.ds(col, width)]
                          .rearrange("(k p) c -> p k c", p=P)).then_inc(sems[f"raw_in{s}"], 16)
            c.advance("block")

        def sp_ada(c, layer, tile):
            for i in range(2):
                c.e.wait_ge(sems["ada_done"], c.next("ada_done"))
                c.e.sem_inc(sems["unused"], 1)
                c.e.dma_start(ada_w[:, i, :].rearrange("p (k c) -> p k c", k=KD),
                              a["w_ada"][layer, :, bass.ds((tile + i) * P, P)]
                              .rearrange("(k p) c -> p k c", p=P)).then_inc(sems[f"ada_in{i}"], 16)

        def act_split(c):
            n = c.static("block")
            c.e.wait_ge(sems[f"raw_in{n % 4}"], c.next(f"raw_in{n % 4}"))
            c.e.wait_ge(sems["tile_done"], c.value("block"))
            c.e.activation(w_hi[:, n % 2, :], raw[:, n % 4, :], ACT.Copy).then_inc(sems["hi_done"], 1)
            c.advance("block")

        def dve_split(c):
            n = c.static("block")
            c.e.wait_ge(sems["hi_done"], c.next("hi_done"))
            c.e.tensor_tensor(w_lo[:, n % 2, :], raw[:, n % 4, :], w_hi[:, n % 2, :].bitcast(F32),
                              ALU.subtract).then_inc(sems["lo_done"], 1)
            c.advance("block")

        def pe_tile(c, rhs_hi, rhs_lo, nk, c0):
            n = c.static("block")
            b, s = n % 4, n % 2
            c.e.wait_ge(sems["lo_done"], c.next("lo_done"))
            c.e.wait_ge(sems[f"free{b}"], c.next(f"free{b}"))
            for k in range(nk):
                hi, lo = w_hi[:, s, k * P:(k + 1) * P], w_lo[:, s, k * P:(k + 1) * P]
                o = ps[:, b, c0:TOK]
                c.e.matmul(o, hi, rhs_hi[:, k, c0:TOK], start=(k == 0), stop=False)
                c.e.matmul(o, hi, rhs_lo[:, k, c0:TOK], start=False, stop=False)
                last = c.e.matmul(o, lo, rhs_hi[:, k, c0:TOK], start=False, stop=(k == nk - 1))
            last.then_inc(sems["tile_done"], 1)
            c.advance("block")

        def pe_ada(c):
            c.e.wait_ge(sems["free7"], c.next("free7"))
            for i in range(2):
                c.e.wait_ge(sems[f"ada_in{i}"], c.next(f"ada_in{i}"))
                for k in range(KD):
                    last = c.e.matmul(ps[:, 7, 2 * i:2 * i + 2], ada_w[:, i, k * P:(k + 1) * P], cT[:, :, k],
                                      start=(k == 0), stop=(k == KD - 1))
                last.then_inc(sems["ada_done"], 1)

        def dve_ada(c, tile):
            c.e.wait_ge(sems["ada_done"], c.next("ada_done"))
            c.e.wait_ge(sems["ada_done"], c.next("ada_done"))
            c.e.tensor_tensor(mod[:, bass.ds(tile, 2), :], ps[:, 7, 0:4].rearrange("p (t s) -> p t s", t=2),
                              bada[:, bass.ds(tile, 2)].rearrange("p (t s) -> p t s", s=1).to_broadcast([P, 2, 2]),
                              ALU.add).then_inc(sems["free7"], 1)

        def tile_wait(c):
            n = c.static("tile")
            c.advance("tile")
            c.e.wait_ge(sems["tile_done"], c.value("tile", plus=1))
            return n % 4

        def act_norm(c, c0):
            c.e.wait_ge(sems["x_ready"], c.next("x_ready"))
            for t in range(KD):
                c.e.wait_ge(sems["sq_used"], c.next("sq_used"))
                c.e.activation(sq[:, t % 2, c0:], xT[:, t, c0:], ACT.Square).then_inc(sems["sqn_ready"], 1)
            act_rstd(c, 4, 0, c0, 1.0 / D, None)
            for t in range(KD):
                c.e.wait_ge(sems["hx_ready"], c.next("hx_ready"))
                c.e.activation(h_hi[:, t, c0:], hx[:, t % 2, c0:], ACT.Copy).then_inc(sems["hhi_ready"], 1)

        def act_rstd(c, b, r, c0, scale, q_bias):
            c.e.wait_ge(sems[f"act{b}"], c.next(f"act{b}"))
            c.e.activation(rstd[:, r, c0:], ps[:, b, c0:TOK], ACT.Ln, bias=bias[:, 0:1], scale=scale) \
               .then_inc(sems[f"free{b}"], 1)
            c.e.drain()
            c.e.activation(rstd[:, r, c0:], rstd[:, r, c0:], ACT.Exp, bias=q_bias if q_bias is not None else 0.0,
                           scale=-0.5).then_inc(sems["rstd_ready"], 1)

        def pe_ssq(c):
            c.e.wait_ge(sems["ssq_ready"], c.next("ssq_ready"))
            c.e.wait_ge(sems["free4"], c.next("free4"))
            c.e.matmul(ps[:, 4, c.c0:TOK], ones, acc[:, c.c0:], start=True, stop=True).then_inc(sems["act4"], 1)

        def dve_norm(c, c0, gain, layer, shift, scale):
            c.e.drain().then_inc(sems["x_ready"], 1)
            if layer is not None:
                s0 = layer * MOD + scale * KD
                c.e.scalar_tensor_tensor(am[:, :, :], mod[:, s0:s0 + KD, :], 1.0,
                                         vec[:, gain:gain + KD].rearrange("p (t s) -> p t s", s=1)
                                         .to_broadcast([P, KD, 2]), ALU.add, ALU.mult)
            for t in range(KD):
                c.e.wait_ge(sems["sqn_ready"], c.next("sqn_ready"))
                if t == 0:
                    c.e.tensor_copy(acc[:, c0:], sq[:, 0, c0:]).then_inc(sems["sq_used"], 1)
                else:
                    c.e.tensor_tensor(acc[:, c0:], acc[:, c0:], sq[:, t % 2, c0:], ALU.add) \
                       .then_inc(sems["sq_used"], 1)
                c.e.drain()
            c.e.drain().then_inc(sems["ssq_ready"], 1)
            c.e.wait_ge(sems["rstd_ready"], c.next("rstd_ready"))
            for t in range(KD + 1):
                if t < KD and layer is not None:
                    b0 = layer * MOD + shift * KD + t
                    c.e.tensor_tensor(hx[:, t % 2, c0:], xT[:, t, c0:], rstd[:, 0, c0:], ALU.mult)
                    c.e.drain()
                    for lo, hi, s in sides[c0]:
                        last = c.e.tensor_scalar(hx[:, t % 2, lo:hi], hx[:, t % 2, lo:hi], am[:, t, s:s + 1],
                                                 mod[:, b0, s:s + 1], ALU.mult, ALU.add)
                        if hi < TOK:
                            continue
                    c.e.drain().then_inc(sems["hx_ready"], 1)
                if t > 0 and layer is not None:
                    c.e.wait_ge(sems["hhi_ready"], c.next("hhi_ready"))
                    c.e.tensor_tensor(h_lo[:, t - 1, c0:], hx[:, (t - 1) % 2, c0:],
                                      h_hi[:, t - 1, c0:].bitcast(F32), ALU.subtract).then_inc(sems["h_ready"], 1)
                    c.e.drain()

        def pe_norm(c, c0):
            c.c0 = c0
            pe_ssq(c)
            for _ in range(KD):
                c.e.wait_ge(sems["h_ready"], c.next("h_ready"))

        def ffn_plan(which):
            first = 0
            for i, n in enumerate(CHUNKS):
                yield i, first, n
                first += n

        def ffn_sp(c, layer, which, ada_from):
            wi, wo = a[f"w_ffn{which}_in"][layer], a[f"w_ffn{which}_out"][layer]
            ada = ada_from
            for i, first, n in ffn_plan(which):
                with c.loop(f"ffn_in{n}{ada is not None}", n // 2) as it:
                    if ada is not None:
                        sp_ada(c, ada // MOD, it * 2 + ada % MOD)
                    for j in range(2):
                        sp_block(c, wi, 0, KD, it * 256 + (first + j) * P)
                        sp_block(c, wi, 0, KD, it * 256 + D_FF + (first + j) * P)
                if ada is not None:
                    ada += n
                with c.loop(f"ffn_out{n}{ada is not None}", 2) as it:
                    if ada is not None:
                        sp_ada(c, ada // MOD, it * 2 + ada % MOD)
                    for j in range(4):
                        sp_block(c, wo, first, n, it * 512 + j * P)
                if ada is not None:
                    ada += 4

        def ffn_pe(c, c0, ada_from):
            ada = ada_from is not None
            for i, first, n in ffn_plan(0):
                with c.loop(f"ffn_in{n}{ada}", n // 2):
                    if ada:
                        pe_ada(c)
                    for j in range(4):
                        pe_tile(c, h_hi, h_lo, KD, c0)
                for _ in range(n):
                    c.e.wait_ge(sems["hid_ready"], c.next("hid_ready"))
                with c.loop(f"ffn_out{n}{ada}", 2):
                    if ada:
                        pe_ada(c)
                    for j in range(4):
                        pe_tile(c, hid_hi, hid_lo, n, c0)

        def ffn_act(c, c0, ada_from, final):
            ada = ada_from is not None
            for i, first, n in ffn_plan(0):
                with c.loop(f"ffn_in{n}{ada}{c0}", n // 2) as it:
                    for j in range(2):
                        act_split(c)
                        b = tile_wait(c)
                        c.e.activation(sil[:, j, c0:], ps[:, b, c0:TOK], ACT.Silu).then_inc(sems["sil_ready"], 1)
                        act_split(c)
                        tile_wait(c)
                        c.e.wait_ge(sems["hprod_ready"], c.next("hprod_ready"))
                        c.e.activation(hid_hi[:, bass.ds(it * 2 + j, 1), c0:], hprod[:, j:j + 1, c0:], ACT.Copy) \
                           .then_inc(sems["hidhi_ready"], 1)
                if final and i == len(CHUNKS) - 1:
                    for j in range(8):
                        if j < 7:
                            act_split(c)
                        c.advance("tile")
                else:
                    with c.loop(f"ffn_out{n}{ada}{c0}", 2):
                        for j in range(4):
                            act_split(c)
                            c.advance("tile")

        def ffn_dve(c, c0, layer, gate_at, ada_from, final):
            ada = ada_from
            for i, first, n in ffn_plan(0):
                with c.loop(f"ffn_in{n}{ada is not None}{c0}", n // 2) as it:
                    for j in range(2):
                        dve_split(c)
                        bg = tile_wait(c)
                        if ada is not None and j == 0:
                            dve_ada(c, it * 2 + ada)
                        dve_split(c)
                        bu = tile_wait(c)
                        c.e.wait_ge(sems["sil_ready"], c.next("sil_ready"))
                        c.e.tensor_tensor(hprod[:, j, c0:], sil[:, j, c0:], ps[:, bu, c0:TOK], ALU.mult) \
                           .then_inc(sems["hprod_ready"], 1)
                        c.e.drain().then_inc(sems[f"free{bg}"], 1)
                        c.e.drain().then_inc(sems[f"free{bu}"], 1)
                        c.e.wait_ge(sems["hidhi_ready"], c.next("hidhi_ready"))
                        c.e.tensor_tensor(hid_lo[:, bass.ds(it * 2 + j, 1), c0:], hprod[:, j:j + 1, c0:],
                                          hid_hi[:, bass.ds(it * 2 + j, 1), c0:].bitcast(F32),
                                          ALU.subtract).then_inc(sems["hid_ready"], 1)
                if ada is not None:
                    ada += n
                if i == 0:
                    g0 = layer * MOD + gate_at * KD
                    c.e.tensor_scalar(gate[:, :, :], mod[:, g0:g0 + KD, :], 0.5, None, ALU.mult)
                    c.e.drain()

                def out_tile(f, split):
                    if split:
                        dve_split(c)
                    b = tile_wait(c)
                    for lo, hi, s in sides[c0]:
                        xs = xT[:, bass.ds(f, 1), lo:hi].rearrange("p a b -> p (a b)")
                        gs = gate[:, bass.ds(f, 1), s:s + 1].rearrange("p a b -> p (a b)")
                        last = c.e.scalar_tensor_tensor(xs, ps[:, b, lo:hi], gs, xs, ALU.mult, ALU.add)
                    last.then_inc(sems[f"free{b}"], 1)

                if final and i == len(CHUNKS) - 1:
                    for j in range(8):
                        out_tile(j, j < 7)
                else:
                    with c.loop(f"ffn_out{n}{ada is not None}{c0}", 2) as it:
                        for j in range(4):
                            out_tile(it * 4 + j, True)
                            if ada is not None and j == 0:
                                dve_ada(c, it * 2 + ada)
                    if ada is not None:
                        ada += 4

        def proj_sp(c, layer, ada_from):
            w = a["w_in"][layer]
            for j in range(4):
                sp_block(c, w, 0, KD, W_Q + j * P)
            sp_block(c, w, 0, KD, W_K)
            sp_block(c, w, 0, KD, W_V)
            sp_block(c, w, 0, KD, W_AB, 16)
            with c.loop(f"qkv{ada_from is not None}", 3) as it:
                if ada_from is not None:
                    sp_ada(c, ada_from // MOD, it * 2 + ada_from % MOD)
                for j in range(4):
                    sp_block(c, w, 0, KD, it * 512 + W_QKV + j * P)

        def proj_pe(c, layer, c0, ada_from):
            for j in range(4):
                pe_tile(c, h_hi, h_lo, KD, c0)
            pe_tile(c, h_hi, h_lo, KD, 0)
            pe_tile(c, h_hi, h_lo, KD, 0)
            n = c.static("block")
            b, s = n % 4, n % 2
            c.e.wait_ge(sems["lo_done"], c.next("lo_done"))
            c.e.wait_ge(sems[f"free{b}"], c.next(f"free{b}"))
            for t in range(4):
                cols = slice(t * P, (t + 1) * P)
                o = ps[:, b, t * 16:(t + 1) * 16]
                for k in range(KD):
                    hi, lo = w_hi[:, s, k * 16:(k + 1) * 16], w_lo[:, s, k * 16:(k + 1) * 16]
                    c.e.matmul(o, h_hi[:, k, cols], hi, start=(k == 0), stop=False)
                    c.e.matmul(o, h_hi[:, k, cols], lo, start=False, stop=False)
                    last = c.e.matmul(o, h_lo[:, k, cols], hi, start=False, stop=(k == KD - 1))
            last.then_inc(sems["tile_done"], 1)
            c.advance("block")
            with c.loop(f"qkv{ada_from is not None}", 3):
                if ada_from is not None:
                    pe_ada(c)
                for j in range(4):
                    pe_tile(c, h_hi, h_lo, KD, 0)
            c.e.wait_ge(sems["kv_ready"], c.next("kv_ready"))
            for h in range(KV_HEADS):
                for r in range(2):
                    b = 4 + r
                    c.e.wait_ge(sems[f"free{b}"], c.next(f"free{b}"))
                    o = C_KD + (2 * h + r) * P
                    c.e.matmul(ps[:, b, (LAT if r else 0):TOK], con[:, o:o + P], kv[:, 0, (LAT if r else 0):],
                               start=True, stop=True).then_inc(sems[f"dve{b}"], 1)
            c.e.wait_ge(sems["free6"], c.next("free6"))
            for t in range(4):
                last = c.e.transpose(ps[:, 6, t * P:(t + 1) * P], kv[:, 1, t * P:(t + 1) * P], ident)
            last.then_inc(sems["act6"], 1)

        def proj_act(c, layer, c0, ada_from):
            for j in range(4):
                act_split(c)
                b = tile_wait(c)
                c.e.activation(attnT[:, j, c0:], ps[:, b, c0:TOK], ACT.Copy).then_inc(sems[f"free{b}"], 1)
            c.e.drain().then_inc(sems["qraw_ready"], 1)
            for j in range(2):
                act_split(c)
                b = tile_wait(c)
                c.e.activation(kv[:, j, :], ps[:, b, :], ACT.Copy).then_inc(sems[f"free{b}"], 1)
            c.e.drain().then_inc(sems["kv_ready"], 1)
            act_split(c)
            c.advance("tile")
            with c.loop(f"qkv{c0}", 3) as it:
                for j in range(4):
                    act_split(c)
                    b = tile_wait(c)
                    c.e.wait_ge(sems["pad_used"], c.next("pad_used"))
                    c.e.activation(pad[:, j % 2, :, PAD:PAD + SEG],
                                   ps[:, b, :].rearrange("p (s t) -> p s t", s=2), ACT.Copy) \
                       .then_inc(sems["pad_ready"], 1)
                    c.e.drain().then_inc(sems[f"free{b}"], 1)
            c.advance("pad_used", 2)
            c.e.wait_ge(sems["act6"], c.next("act6"))
            c.e.activation(vnat[:, :, :], bank4(6), ACT.Copy).then_inc(sems["free6"], 1)
            c.e.drain().then_inc(sems["kd_ready"], 1)

        def proj_dve(c, layer, c0, ada_from):
            c.e.memset(pad[:, :, :, 0:PAD], 0.0)
            c.e.memset(pad[:, :, :, PAD + SEG:], 0.0)
            for _ in range(2):
                c.e.drain().then_inc(sems["pad_used"], 1)
            for j in range(6):
                dve_split(c)
                c.advance("tile")
            dve_split(c)
            b = tile_wait(c)
            ab = ps[:, b, 0:64].rearrange("p (t d h) -> p d t h", t=4, h=GH)
            for d in range(2):
                c.e.tensor_tensor(gtmp[:, 0, d], ab[:, d],
                                  dtb[:, layer, d:d + 1, :].to_broadcast([P, 4, GH]), ALU.add)
                c.e.tensor_scalar(beta[:, d], ab[:, 2 + d], -1.0, None, ALU.mult)
            c.e.drain().then_inc(sems[f"free{b}"], 1)
            c.e.tensor_scalar(gtmp[:, 2], gtmp[:, 0], -1.0, None, ALU.mult)
            c.e.drain()
            c.e.tensor_tensor(gtmp[:, 1], gtmp[:, 2], gtmp[:, 0], ALU.min)
            c.e.drain().then_inc(sems["ab_ready"], 1)
            with c.loop(f"qkv{c0}{ada_from is not None}", 3) as it:
                for j in range(4):
                    dve_split(c)
                    c.advance("tile")
                    if ada_from is not None and j == 0:
                        dve_ada(c, it * 2 + ada_from)
                    c.e.wait_ge(sems["pad_ready"], c.next("pad_ready"))
                    o = qkvT[:, bass.ds(it * 4 + j, 1), :].rearrange("p a (s t) -> p (a s) t", s=2)

                    def cw(tap):
                        return convw[:, layer, tap, bass.ds(it * 4 + j, 1)]

                    c.e.tensor_scalar(o, pad[:, j % 2, :, 0:SEG], cw(0), None, ALU.mult)
                    for tap in range(1, CONV):
                        c.e.drain()
                        last = c.e.scalar_tensor_tensor(o, pad[:, j % 2, :, tap:tap + SEG], cw(tap), o,
                                                        ALU.mult, ALU.add)
                    last.then_inc(sems["pad_used"], 1)
            c.e.drain().then_inc(sems["conv_ready"], 1)
            for h in range(KV_HEADS):
                c.e.wait_ge(sems["dve4"], c.next("dve4"))
                c.e.tensor_copy(kd[:, h, 0:LAT], ps[:, 4, 0:LAT])
                c.e.tensor_tensor(rtmp[:, 0, :], ps[:, 4, LAT:TOK], con[:, C_COS:C_COS + SEG], ALU.mult) \
                   .then_inc(sems["free4"], 1)
                c.e.wait_ge(sems["dve5"], c.next("dve5"))
                c.e.tensor_tensor(rtmp[:, 1, :], ps[:, 5, LAT:TOK], con[:, C_SIN:C_SIN + SEG], ALU.mult) \
                   .then_inc(sems["free5"], 1)
                c.e.drain()
                c.e.tensor_tensor(kd[:, h, LAT:TOK], rtmp[:, 0, :], rtmp[:, 1, :], ALU.add)
                c.e.drain()
            c.e.wait_ge(sems["kd_ready"], c.next("kd_ready"))

        def att_items(c0):
            return [(kvh, hh, qt) for kvh in range(2) for hh in range(2) for qt in range(c0 // P, 4)]

        def att_pe(c, c0):
            items = att_items(c0)
            n = len(items)
            with c.loop(f"att{c0}", 2) as it:
                for kvh in range(2):
                    c.e.wait_ge(sems["free4"], c.next("free4"))
                    c.e.matmul(ps[:, 4, LAT:TOK], con[:, C_ROT:C_ROT + P],
                               attnT[:, bass.ds(it + 2 * kvh, 1), LAT:], start=True, stop=True) \
                       .then_inc(sems["dve4"], 1)
                for k in range(n + 3):
                    if k < n:
                        kvh, hh, qt = items[k]
                        if k == 0 or items[k - 1][0] != kvh:
                            c.e.wait_ge(sems["qs_ready"], c.next("qs_ready"))
                        b = k % 2
                        c.e.wait_ge(sems[f"free{b}"], c.next(f"free{b}"))
                        p = slice(64 * hh, 64 * hh + 64)
                        nk = TOK if qt >= 2 else SEG
                        c.e.matmul(ps[:, b, 0:nk], qs[p, kvh, qt * P:(qt + 1) * P], kd[p, kvh, 0:nk],
                                   start=True, stop=True).then_inc(sems[f"dve{b}"], 1)
                    if 0 <= k - 2 < n:
                        i = k - 2
                        b = 2 + i % 2
                        c.e.wait_ge(sems["p_ready"], c.next("p_ready"))
                        c.e.wait_ge(sems[f"free{b}"], c.next(f"free{b}"))
                        for kb in range(4 if items[i][2] >= 2 else 2):
                            last = c.e.transpose(ps[:, b, kb * P:(kb + 1) * P], sc[:, i % 3, kb * P:(kb + 1) * P],
                                                 ident)
                        last.then_inc(sems[f"act{b}"], 1)
                    if 0 <= k - 3 < n:
                        i = k - 3
                        kvh, hh, qt = items[i]
                        b = 5 + i % 2
                        c.e.wait_ge(sems["pT_ready"], c.next("pT_ready"))
                        c.e.wait_ge(sems[f"free{b}"], c.next(f"free{b}"))
                        nb = 4 if qt >= 2 else 2
                        for kb in range(nb):
                            last = c.e.matmul(ps[64 * hh:64 * hh + 64, b, 0:P], vnat[:, kb, 64 * kvh:64 * kvh + 64],
                                              pT[:, i % 2, kb, :], start=(kb == 0), stop=(kb == nb - 1))
                        last.then_inc(sems[f"dve{b}"], 1)

        def att_dve(c, c0, layer):
            items = att_items(c0)
            n = len(items)
            c.e.wait_ge(sems["qraw_ready"], c.next("qraw_ready"))
            with c.loop(f"att{c0}", 2) as it:
                for kvh in range(2):
                    q = attnT[:, bass.ds(it + 2 * kvh, 1), :].rearrange("p a b -> p (a b)")
                    if c0 == 0:
                        c.e.tensor_copy(qs[:, kvh, 0:LAT], attnT[:, bass.ds(it + 2 * kvh, 1), 0:LAT]
                                        .rearrange("p a b -> p (a b)"))
                    c.e.tensor_tensor(rtmp[:, 0, :], attnT[:, bass.ds(it + 2 * kvh, 1), LAT:]
                                      .rearrange("p a b -> p (a b)"), con[:, C_COS:C_COS + SEG], ALU.mult)
                    c.e.wait_ge(sems["dve4"], c.next("dve4"))
                    c.e.tensor_tensor(rtmp[:, 1, :], ps[:, 4, LAT:TOK], con[:, C_SIN:C_SIN + SEG], ALU.mult) \
                       .then_inc(sems["free4"], 1)
                    c.e.drain()
                    c.e.tensor_tensor(qs[:, kvh, LAT:], rtmp[:, 0, :], rtmp[:, 1, :], ALU.add)
                    c.e.drain().then_inc(sems["qs_ready"], 1)
                for k in range(n + 3):
                    if k < n:
                        kvh, hh, qt = items[k]
                        b, r = k % 2, k % 3
                        nk = TOK if qt >= 2 else SEG
                        hc = bass.ds(it * 2 + 4 * kvh + hh, 1)
                        c.e.wait_ge(sems[f"dve{b}"], c.next(f"dve{b}"))
                        if qt >= 2:
                            mk = con[:, C_MASK + (qt - 2) * TOK:C_MASK + (qt - 1) * TOK]
                            c.e.scalar_tensor_tensor(sc[:, r, :], ps[:, b, :], DH ** -0.5, mk, ALU.mult, ALU.add) \
                               .then_inc(sems[f"free{b}"], 1)
                        else:
                            c.e.tensor_scalar(sc[:, r, 0:nk], ps[:, b, 0:nk], DH ** -0.5, None, ALU.mult) \
                               .then_inc(sems[f"free{b}"], 1)
                        c.e.drain()
                        c.e.tensor_reduce(stat[:, k % 4, 0:1], sc[:, r, 0:nk], AX.X, ALU.max)
                        c.e.drain()
                        c.e.tensor_scalar(stat[:, k % 4, 1:2], stat[:, k % 4, 0:1], sink[:, layer, hc], -1.0,
                                          ALU.max, ALU.mult).then_inc(sems["sc_ready"], 1)
                    if 0 <= k - 1 < n:
                        i = k - 1
                        nk = TOK if items[i][2] >= 2 else SEG
                        st = stat[:, i % 4, :]
                        c.e.wait_ge(sems["exp_ready"], c.next("exp_ready"))
                        c.e.tensor_tensor(st[:, 4:5], st[:, 2:3], st[:, 3:4], ALU.add)
                        c.e.drain()
                        c.e.reciprocal(st[:, 5:6], st[:, 4:5])
                        c.e.drain()
                        c.e.tensor_scalar(sc[:, i % 3, 0:nk], sc[:, i % 3, 0:nk], st[:, 5:6], None, ALU.mult) \
                           .then_inc(sems["p_ready"], 1)
                    if 0 <= k - 3 < n:
                        i = k - 3
                        kvh, hh, qt = items[i]
                        b = 5 + i % 2
                        p = slice(64 * hh, 64 * hh + 64)
                        c.e.wait_ge(sems[f"dve{b}"], c.next(f"dve{b}"))
                        c.e.tensor_scalar(attnT[p, bass.ds(it + 2 * kvh, 1), qt * P:(qt + 1) * P],
                                          ps[p, b, 0:P].rearrange("p (a b) -> p a b", a=1), 1.0, None, ALU.mult) \
                           .then_inc(sems[f"free{b}"], 1)
                c.e.drain()

        def att_act(c, c0, layer):
            items = att_items(c0)
            n = len(items)
            with c.loop(f"att{c0}", 2) as it:
                for k in range(n + 2):
                    if k < n:
                        kvh, hh, qt = items[k]
                        nk = TOK if qt >= 2 else SEG
                        st = stat[:, k % 4, :]
                        hc = bass.ds(it * 2 + 4 * kvh + hh, 1)
                        c.e.wait_ge(sems["sc_ready"], c.next("sc_ready"))
                        c.e.activation(sc[:, k % 3, 0:nk], sc[:, k % 3, 0:nk], ACT.Exp, bias=st[:, 1:2],
                                       accum_out=st[:, 2:3])
                        c.e.activation(st[:, 3:4], sink[:, layer, hc], ACT.Exp, bias=st[:, 1:2])
                        c.e.drain().then_inc(sems["exp_ready"], 1)
                    if 0 <= k - 2 < n:
                        i = k - 2
                        b = 2 + i % 2
                        nb = 4 if items[i][2] >= 2 else 2
                        c.e.wait_ge(sems[f"act{b}"], c.next(f"act{b}"))
                        c.e.activation(pT[:, i % 2, 0:nb, :], bank4(b)[:, 0:nb, :], ACT.Copy) \
                           .then_inc(sems["pT_ready"], 1)
                        c.e.drain().then_inc(sems[f"free{b}"], 1)

        def qk_act(c):
            c.e.wait_ge(sems["conv_ready"], c.next("conv_ready"))
            for t in range(3):
                c.e.activation(qkvT[:, 4 * t:4 * t + 4, :], qkvT[:, 4 * t:4 * t + 4, :], ACT.Silu)
                c.e.drain()
            c.e.drain().then_inc(sems["silu_ready"], 1)
            c.e.wait_ge(sems["ab_ready"], c.next("ab_ready"))
            c.e.activation(gtmp[:, 1], gtmp[:, 1], ACT.Exp)
            c.e.activation(beta[:, :], beta[:, :], ACT.Exp)
            c.e.activation(gtmp[:, 2, :, 0, :], alog[:, c.layer], ACT.Exp)
            c.e.drain()
            c.e.activation(gtmp[:, 1], gtmp[:, 1], ACT.Ln, bias=bias[:, 2:3])
            c.e.drain().then_inc(sems["abexp_ready"], 1)
            with c.loop("qknorm", 4) as it:
                for j in range(2):
                    c.e.wait_ge(sems["sq_used"], c.next("sq_used"))
                    c.e.activation(sq[:, j:j + 1, :], qkvT[:, bass.ds(it + 4 * j, 1), :], ACT.Square) \
                       .then_inc(sems["sq_ready"], 1)
                for j in range(2):
                    act_rstd(c, 4 + j, j, 0, 1.0, bias[:, 1:2] if j == 0 else None)
            c.e.wait_ge(sems["act6"], c.next("act6"))
            c.e.activation(gcn[:, :, :, :], ps[:, 6, 0:32].rearrange("p (d t h) -> p d t h", d=2, h=GH), ACT.Copy)
            c.e.activation(negeg[:, :, :, :], ps[:, 6, 0:32].rearrange("p (d t h) -> p d t h", d=2, h=GH), ACT.Exp)
            c.e.activation(gtot[:, :, :, :], ps[:, 6, 32:64].rearrange("p (d t h) -> p d t h", d=2, h=GH), ACT.Exp)
            c.e.drain().then_inc(sems["gcx_ready"], 1)
            c.e.wait_ge(sems["act_go"], c.next("act_go"))
            c.e.activation(dec[:, :, :, :], dec[:, :, :, :], ACT.Exp)
            c.e.drain().then_inc(sems["gcx_ready"], 1)

        def qk_pe(c):
            with c.loop("qknorm", 4):
                for j in range(2):
                    c.e.wait_ge(sems["sq_ready"], c.next("sq_ready"))
                    c.e.wait_ge(sems[f"free{4 + j}"], c.next(f"free{4 + j}"))
                    c.e.matmul(ps[:, 4 + j, :], ones, sq[:, j, :], start=True, stop=True) \
                       .then_inc(sems[f"act{4 + j}"], 1)
            c.e.wait_ge(sems["g_ready"], c.next("g_ready"))
            c.e.wait_ge(sems["free6"], c.next("free6"))
            for d in range(2):
                c.e.matmul(ps[:, 6, 16 * d:16 * d + 16], tri(d), gates[:, d], start=True, stop=True)
            c.e.matmul(ps[:, 6, 32:64], ones, gates[:, :, :, :].rearrange("p d t h -> p (d t h)"),
                       start=True, stop=True).then_inc(sems["act6"], 1)

        def qk_dve(c, layer):
            c.e.wait_ge(sems["silu_ready"], c.next("silu_ready"))
            with c.loop("qknorm", 4) as it:
                for j in range(2):
                    c.e.wait_ge(sems["rstd_ready"], c.next("rstd_ready"))
                    q = qkvT[:, bass.ds(it + 4 * j, 1), :]
                    c.e.tensor_tensor(q, q, rstd[:, j:j + 1, :], ALU.mult).then_inc(sems["sq_used"], 1)
            c.e.wait_ge(sems["abexp_ready"], c.next("abexp_ready"))
            c.e.scalar_tensor_tensor(gtmp[:, 0], gtmp[:, 0], 0.0, gtmp[:, 1], ALU.max, ALU.add)
            c.e.tensor_scalar(beta[:, :], beta[:, :], 1.0, None, ALU.add)
            c.e.drain()
            for d in range(2):
                c.e.scalar_tensor_tensor(gates[:, d], gtmp[:, 0, d], -1.0,
                                         gtmp[:, 2, d, 0:1, :].to_broadcast([P, 4, GH]), ALU.mult, ALU.mult)
            c.e.reciprocal(beta[:, :], beta[:, :])
            c.e.drain().then_inc(sems["g_ready"], 1)
            c.e.wait_ge(sems["gcx_ready"], c.next("gcx_ready"))
            c.e.tensor_tensor(dec[:, :, :, :], ps[:, 6, 32:64].rearrange("p (d t h) -> p d t h", d=2, h=GH),
                              gcn[:, :, :, :], ALU.subtract)
            c.e.tensor_scalar(negeg[:, :, :, :], negeg[:, :, :, :], -1.0, None, ALU.mult)
            c.e.drain().then_inc(sems["free6"], 1)
            c.e.drain().then_inc(sems["act_go"], 1)
            c.e.wait_ge(sems["gcx_ready"], c.next("gcx_ready"))
            c.e.memset(state[:, :, :, :], 0.0)
            c.e.drain().then_inc(sems["stage_free"], 1)

        def steps():
            return [(step, d) for step in range(2) for d in range(2)]

        def tile_of(it, step, d):
            return it * 2 + (step if d == 0 else 1 - step)

        def gdn_pool(c):
            with c.loop("gdn", 2) as it:
                for step in range(2):
                    c.e.wait_ge(sems["stage_free"], c.next("stage_free"))
                    c.e.sem_inc(sems["unused"], 1)
                    for d in range(2):
                        cols = bass.ds(tile_of(it, step, d) * P, P)
                        c.e.tensor_copy(G[:, d, QS], qkvT[:, 0:4, cols])
                        c.e.tensor_copy(G[:, d, KTS], qkvT[:, 4:8, cols])
                        c.e.tensor_copy(G[:, d, UU], qkvT[:, 8:12, cols]).then_inc(sems["staged"], 1)

        def mm4(c, b, f, to="dve"):
            c.e.wait_ge(sems[f"free{b}"], c.next(f"free{b}"))
            for h in range(GH):
                last = f(h, ps[:, b, h * P:(h + 1) * P])
            last.then_inc(sems[f"{to}{b}"], 1)

        def gdn_pe(c):
            mm = c.e.matmul
            with c.loop("gdn", 2):
                for step in range(2):
                    for d in range(2):
                        g = G[:, d]
                        c.e.wait_ge(sems["staged"], c.next("staged"))
                        mm4(c, 3 * d, lambda h, o: c.e.transpose(o, g[:, UU, h], ident), "act")
                    for d in range(2):
                        g = G[:, d]
                        c.e.wait_ge(sems["pe_go"], c.next("pe_go"))
                        b = 3 * d + 1
                        c.e.wait_ge(sems[f"free{b}"], c.next(f"free{b}"))
                        mm(ps[:, b, :], ones, g[:, PP].rearrange("p h c -> p (h c)"), start=True, stop=True) \
                            .then_inc(sems[f"dve{b}"], 1)
                    for d in range(2):
                        g = G[:, d]
                        mm4(c, 3 * d + 2, lambda h, o: mm(o, g[:, KTS, h], g[:, KTS, h], start=True, stop=True))
                        mm4(c, 3 * d, lambda h, o: mm(o, g[:, KTS, h], g[:, QS, h], start=True, stop=True))
                    for d in range(2):
                        g = G[:, d]
                        c.e.wait_ge(sems["pe_go"], c.next("pe_go"))
                        mm4(c, 3 * d + 1, lambda h, o: c.e.transpose(o, g[:, UU, h], ident))
                    for s in range(1, LEVELS):
                        for d in range(2):
                            g = G[:, d]
                            c.e.wait_ge(sems["pe_go"], c.next("pe_go"))
                            mm4(c, 3 * d, lambda h, o: mm(o, g[:, NM, h], g[:, TT, h], start=True, stop=True), "act")
                        for d in range(2):
                            g = G[:, d]
                            c.e.wait_ge(sems["p_copied"], c.next("p_copied"))
                            if s < LEVELS - 1:
                                mm4(c, 3 * d + 1, lambda h, o: mm(o, g[:, UU, h], g[:, PP, h], start=True, stop=True))
                            mm4(c, 3 * d + 2, lambda h, o: mm(o, g[:, PP, h], g[:, UU, h], start=True, stop=True))
                    for d in range(2):
                        g = G[:, d]
                        c.e.wait_ge(sems["pe_go"], c.next("pe_go"))
                        mm4(c, 3 * d, lambda h, o: c.e.transpose(o, g[:, KTS, h], ident), "act")
                        mm4(c, 3 * d + 1, lambda h, o: mm(o, g[:, KTS, h], state[:, d, h], start=True, stop=True))
                    for d in range(2):
                        g = G[:, d]
                        c.e.wait_ge(sems["pe_go"], c.next("pe_go"))
                        mm4(c, 3 * d + 2, lambda h, o: mm(o, g[:, UU, h], g[:, VN, h], start=True, stop=True))
                    for d in range(2):
                        g = G[:, d]
                        c.e.wait_ge(sems["pe_go"], c.next("pe_go"))
                        b = 3 * d
                        c.e.wait_ge(sems[f"free{b}"], c.next(f"free{b}"))
                        for h in range(GH):
                            o = ps[:, b, h * P:(h + 1) * P]
                            mm(o, state[:, d, h], g[:, QS, h], start=True, stop=False)
                            last = mm(o, g[:, TT, h], g[:, EE, h], start=False, stop=True)
                        last.then_inc(sems[f"dve{b}"], 1)
                        mm4(c, b + 1, lambda h, o: mm(o, g[:, NM, h], g[:, PP, h], start=True, stop=True))

        def gdn_act(c):
            with c.loop("gdn", 2):
                for step in range(2):
                    for d in range(2):
                        c.e.wait_ge(sems[f"act{3 * d}"], c.next(f"act{3 * d}"))
                        c.e.activation(G[:, d, VN], bank4(3 * d), ACT.Copy).then_inc(sems[f"free{3 * d}"], 1)
                    for d in range(2):
                        c.e.wait_ge(sems["act_go"], c.next("act_go"))
                        c.e.activation(G[:, d, EE], G[:, d, EE], ACT.Exp)
                        c.e.activation(G[:, d, TT], bank4(3 * d + 1), ACT.Exp).then_inc(sems[f"free{3 * d + 1}"], 1)
                        c.e.drain().then_inc(sems["e_ready"], 1)
                    for s in range(1, LEVELS):
                        for d in range(2):
                            c.e.wait_ge(sems[f"act{3 * d}"], c.next(f"act{3 * d}"))
                            c.e.activation(G[:, d, PP], bank4(3 * d), ACT.Copy).then_inc(sems["p_copied"], 1)
                            c.e.drain().then_inc(sems[f"free{3 * d}"], 1)
                    for d in range(2):
                        c.e.wait_ge(sems[f"act{3 * d}"], c.next(f"act{3 * d}"))
                        c.e.activation(G[:, d, NM], bank4(3 * d), ACT.Copy).then_inc(sems[f"free{3 * d}"], 1)
                    c.e.drain().then_inc(sems["e_ready"], 1)

        def gdn_dve(c):
            with c.loop("gdn", 2) as it:
                for step in range(2):
                    gt = [bass.ds(tile_of(it, step, d), 1) for d in range(2)]

                    def col(buf, d, h):
                        return buf[:, d, gt[d], h:h + 1].rearrange("p a b -> p (a b)")

                    for d in range(2):
                        g = G[:, d]
                        c.e.wait_ge(sems[f"staged"], c.next(f"staged"))
                        c.e.tensor_tensor(g[:, PP], heads(tri(d)),
                                          gates[:, d, gt[d], :].rearrange("p a h -> p h a").to_broadcast([P, GH, P]),
                                          ALU.mult).then_inc(sems["pe_go"], 1)
                    for d in range(2):
                        g = G[:, d]
                        b = 3 * d + 1
                        c.e.wait_ge(sems[f"dve{b}"], c.next(f"dve{b}"))
                        for h in range(GH):
                            last = c.e.scalar_tensor_tensor(g[:, EE, h], ps[:, b, h * P:(h + 1) * P], col(gcn, d, h),
                                                            negm(d), ALU.subtract, ALU.add)
                        last.then_inc(sems["act_go"], 1)
                    for d in range(2):
                        g = G[:, d]
                        c.e.wait_ge(sems["e_ready"], c.next("e_ready"))
                        b = 3 * d + 2
                        c.e.wait_ge(sems[f"dve{b}"], c.next(f"dve{b}"))
                        for h in range(GH):
                            last = c.e.scalar_tensor_tensor(g[:, NT, h], ps[:, b, h * P:(h + 1) * P],
                                                            col(beta, d, h), g[:, EE, h], ALU.mult, ALU.mult)
                        last.then_inc(sems[f"free{b}"], 1)
                        c.e.drain()
                        c.e.wait_ge(sems[f"dve{3 * d}"], c.next(f"dve{3 * d}"))
                        c.e.tensor_tensor(g[:, EE], bank4(3 * d), g[:, EE], ALU.mult).then_inc(sems[f"free{3 * d}"], 1)
                        c.e.tensor_tensor(g[:, QS], g[:, QS], g[:, TT], ALU.mult)
                        c.e.drain()
                        c.e.tensor_tensor(g[:, UU], g[:, NT], heads(lev(d, 0)), ALU.mult)
                        c.e.drain()
                        c.e.scalar_tensor_tensor(g[:, UU], g[:, UU], -1.0, heads(ident), ALU.mult, ALU.add) \
                           .then_inc(sems["pe_go"], 1)
                    for s in range(1, LEVELS):
                        for d in range(2):
                            g = G[:, d]
                            c.e.tensor_tensor(g[:, NM], g[:, NT], heads(lev(d, s)), ALU.mult)
                            if s == 1:
                                c.e.wait_ge(sems[f"dve{3 * d + 1}"], c.next(f"dve{3 * d + 1}"))
                                c.e.tensor_copy(g[:, TT], bank4(3 * d + 1)).then_inc(sems[f"free{3 * d + 1}"], 1)
                            c.e.drain().then_inc(sems["pe_go"], 1)
                        for d in range(2):
                            g = G[:, d]
                            if s < LEVELS - 1:
                                b = 3 * d + 1
                                c.e.wait_ge(sems[f"dve{b}"], c.next(f"dve{b}"))
                                c.e.tensor_tensor(g[:, TT], g[:, TT], bank4(b), ALU.subtract) \
                                   .then_inc(sems[f"free{b}"], 1)
                            b = 3 * d + 2
                            c.e.wait_ge(sems[f"dve{b}"], c.next(f"dve{b}"))
                            c.e.tensor_tensor(g[:, UU], g[:, UU], bank4(b), ALU.subtract).then_inc(sems[f"free{b}"], 1)
                            c.e.drain()
                    for d in range(2):
                        c.e.drain().then_inc(sems["pe_go"], 1)
                    for d in range(2):
                        g = G[:, d]
                        b = 3 * d + 1
                        c.e.wait_ge(sems[f"dve{b}"], c.next(f"dve{b}"))
                        for h in range(GH):
                            last = c.e.scalar_tensor_tensor(g[:, VN, h], ps[:, b, h * P:(h + 1) * P],
                                                            col(negeg, d, h), g[:, VN, h], ALU.mult, ALU.add)
                        c.e.drain().then_inc(sems[f"free{b}"], 1)
                        c.e.drain().then_inc(sems["pe_go"], 1)
                    c.e.wait_ge(sems["e_ready"], c.next("e_ready"))
                    for d in range(2):
                        g = G[:, d]
                        b = 3 * d + 2
                        c.e.wait_ge(sems[f"dve{b}"], c.next(f"dve{b}"))
                        for h in range(GH):
                            c.e.tensor_scalar(g[:, TT, h], ps[:, b, h * P:(h + 1) * P], col(beta, d, h), None,
                                              ALU.mult)
                            c.e.tensor_scalar(g[:, PP, h], ps[:, b, h * P:(h + 1) * P], col(beta, d, h),
                                              col(dec, d, h), ALU.mult, ALU.mult)
                        c.e.drain().then_inc(sems[f"free{b}"], 1)
                        c.e.drain().then_inc(sems["pe_go"], 1)
                    for d in range(2):
                        g = G[:, d]
                        b = 3 * d
                        o = gdnT[:, :, bass.ds(tile_of(it, step, d) * P, P)]
                        c.e.wait_ge(sems[f"dve{b}"], c.next(f"dve{b}"))
                        if step == 0:
                            c.e.tensor_scalar(o, bank4(b), 1.0, None, ALU.mult).then_inc(sems[f"free{b}"], 1)
                        else:
                            c.e.tensor_tensor(o, o, bank4(b), ALU.add).then_inc(sems[f"free{b}"], 1)
                        b = 3 * d + 1
                        c.e.wait_ge(sems[f"dve{b}"], c.next(f"dve{b}"))
                        for h in range(GH):
                            last = c.e.scalar_tensor_tensor(state[:, d, h], state[:, d, h], col(gtot, d, h),
                                                            ps[:, b, h * P:(h + 1) * P], ALU.mult, ALU.add)
                        last.then_inc(sems[f"free{b}"], 1)
                    c.e.drain().then_inc(sems["stage_free"], 1)
            c.e.drain().then_inc(sems["gdn_over"], 1)

        def late_sp(c, layer, ada_from):
            w = a["w_in"][layer]
            for part, w0 in enumerate((W_ZG, W_PIN)):
                sp_ada(c, (ada_from + 2 * part) // MOD, (ada_from + 2 * part) % MOD)
                for j in range(4):
                    sp_block(c, w, 0, KD, w0 + j * P)
            c.e.wait_ge(sems["z_ready"], c.next("z_ready"))
            c.e.dma_start(pw[:, :, :], a["pool_w"][layer].rearrange("g c d -> c g d")) \
               .then_inc(sems["dma_pw"], 16)

        def late_pe(c, c0):
            pe_ada(c)
            for j in range(4):
                pe_tile(c, h_hi, h_lo, KD, c0)
            pe_ada(c)
            for j in range(4):
                pe_tile(c, h_hi, h_lo, KD, c0)
            for h in range(GH):
                c.e.wait_ge(sems["sq_ready"], c.next("sq_ready"))
                b = 4 + h % 2
                c.e.wait_ge(sems[f"free{b}"], c.next(f"free{b}"))
                c.e.matmul(ps[:, b, c0:TOK], ones, sq[:, h % 2, c0:], start=True, stop=True) \
                   .then_inc(sems[f"act{b}"], 1)
            c.e.wait_ge(sems["dma_pw"], c.next("dma_pw"))
            for g in range(4):
                c.e.wait_ge(sems["pin_ready"], c.next("pin_ready"))
                b = 6
                c.e.wait_ge(sems[f"free{b}"], c.next(f"free{b}"))
                c.e.matmul(ps[:, b, c0:TOK], pw[:, g, :], poolT[:, g, c0:], start=True, stop=True) \
                   .then_inc(sems[f"dve{b}"], 1)

        def late_act(c, c0):
            for j in range(4):
                act_split(c)
                b = tile_wait(c)
                if j == 0:
                    c.e.wait_ge(sems["gdn_over"], c.next("gdn_over"))
                c.e.activation(merged[:, j, c0:], ps[:, b, c0:TOK], ACT.Silu).then_inc(sems[f"free{b}"], 1)
            c.e.drain().then_inc(sems["z_ready"], 1)
            c.e.drain().then_inc(sems["o_ready"], 1)
            for j in range(4):
                act_split(c)
                b = tile_wait(c)
                c.e.wait_ge(sems["pad_used"], c.next("pad_used"))
                n = 2 if c0 == 0 else 1
                c.e.activation(ppad[:, j % 2, 2 - n:2, 8:8 + SEG],
                               ps[:, b, c0:TOK].rearrange("p (s t) -> p s t", s=n), ACT.Copy) \
                   .then_inc(sems["pad_ready"], 1)
                c.e.drain().then_inc(sems[f"free{b}"], 1)
            c.advance("pad_used", 2)
            for h in range(GH):
                c.e.wait_ge(sems["sq_used"], c.next("sq_used"))
                c.e.activation(sq[:, h % 2, c0:], gdnT[:, h, c0:], ACT.Square).then_inc(sems["sq_ready"], 1)
                if h > 0:
                    act_rstd(c, 4 + (h - 1) % 2, (h - 1) % 2, c0, 1.0 / GD, None)
            act_rstd(c, 4 + (GH - 1) % 2, (GH - 1) % 2, c0, 1.0 / GD, None)

        def late_dve(c, c0, layer, ada_from):
            s0 = 0 if c0 == 0 else 1
            for part in range(2):
                for j in range(4):
                    dve_split(c)
                    c.advance("tile")
                    if j == 0:
                        dve_ada(c, ada_from + 2 * part)
                    if part == 0:
                        continue
                    if j == 0:
                        c.e.wait_ge(sems["o_ready"], c.next("o_ready"))
                        c.e.memset(ppad[:, :, :, 0:8], 0.0)
                        c.e.memset(ppad[:, :, :, 8 + SEG:], 0.0)
                        c.e.drain().then_inc(sems["pad_used"], 1)
                        c.e.drain().then_inc(sems["pad_used"], 1)
                    c.e.wait_ge(sems["pad_ready"], c.next("pad_ready"))
                    src = ppad[:, j % 2, s0:2, :]
                    w, n = 1, SEG + 16
                    cur = src
                    for lv in range(j + 1):
                        n -= w
                        nxt = pool_s[:, lv % 2, s0:2, 0:n]
                        c.e.tensor_tensor(nxt, cur[:, :, 0:n], cur[:, :, w:w + n], ALU.add)
                        c.e.drain()
                        cur = nxt
                        w *= 2
                    o = poolT[:, j, c0:].rearrange("p (s t) -> p s t", t=SEG)
                    off = 8 - w // 2
                    c.e.tensor_scalar(o, cur[:, :, off:off + SEG], 1.0 / w, None, ALU.mult)
                    c.e.drain()
                    for e, at in ((0, 0), (1, SEG - 8)):
                        ed = con[:, C_EDGE + (j * 2 + e) * 8:C_EDGE + (j * 2 + e + 1) * 8]
                        c.e.tensor_tensor(o[:, :, at:at + 8], cur[:, :, off + at:off + at + 8],
                                          ed.rearrange("p (s t) -> p s t", s=1).to_broadcast([P, 2 - s0, 8]), ALU.mult)
                    c.e.drain()
                    c.e.tensor_tensor(o, o, src[:, :, 8:8 + SEG], ALU.subtract)
                    c.e.drain().then_inc(sems["pin_ready"], 1)
                    c.e.drain().then_inc(sems["pad_used"], 1)
            for h in range(GH):
                c.e.wait_ge(sems["rstd_ready"], c.next("rstd_ready"))
                c.e.tensor_tensor(gdnT[:, h, c0:], gdnT[:, h, c0:], rstd[:, h % 2, c0:], ALU.mult)
                c.e.drain()
                c.e.scalar_tensor_tensor(gdnT[:, h, c0:], gdnT[:, h, c0:],
                                         vec[:, V_GN + layer:V_GN + layer + 1], merged[:, h, c0:],
                                         ALU.mult, ALU.mult)
                c.e.drain().then_inc(sems["sq_used"], 1)
            for g in range(4):
                c.e.wait_ge(sems["dve6"], c.next("dve6"))
                v = V_PS + layer * 4 + g
                c.e.tensor_scalar(poolT[:, g, c0:], ps[:, 6, c0:TOK], vec[:, v:v + 1], None, ALU.mult) \
                   .then_inc(sems["free6"], 1)
            c.e.drain().then_inc(sems["br_ready"], 1)

        def merge_sp(c, layer, ada_from):
            w = a["w_in"][layer]
            ada = ada_from
            for b, name in enumerate(("w_branch_attn", "w_branch_gdn", "w_branch_pool")):
                with_ada = ada_from is not None and b == 0
                with c.loop(f"merge{with_ada}", 4) as it:
                    if with_ada:
                        sp_ada(c, ada // MOD, it * 2 + ada % MOD)
                    for j in range(2):
                        sp_block(c, w, 0, KD, it * 256 + W_GL + b * D + j * P)
                        sp_block(c, a[name][layer], 0, 4, it * 256 + j * P)
            with_ada = ada_from is not None
            with c.loop(f"wout{with_ada}", 2) as it:
                if with_ada:
                    sp_ada(c, (ada + 8) // MOD, it * 2 + (ada + 8) % MOD)
                for j in range(4):
                    sp_block(c, a["w_out"][layer], 0, KD, it * 512 + j * P)

        def merge_pe(c, c0, ada_from):
            for b in range(3):
                with_ada = ada_from is not None and b == 0
                for _ in range(4):
                    c.e.wait_ge(sems["brlo_ready"], c.next("brlo_ready"))
                with c.loop(f"merge{with_ada}", 4):
                    if with_ada:
                        pe_ada(c)
                    for j in range(2):
                        pe_tile(c, h_hi, h_lo, KD, c0)
                        pe_tile(c, br_hi, br_lo, 4, c0)
            for _ in range(KD):
                c.e.wait_ge(sems["mlo_ready"], c.next("mlo_ready"))
            with_ada = ada_from is not None
            with c.loop(f"wout{with_ada}", 2):
                if with_ada:
                    pe_ada(c)
                for j in range(4):
                    pe_tile(c, h_hi, h_lo, KD, c0)

        def merge_act(c, c0, ada_from):
            for b in range(3):
                src = (attnT, gdnT, poolT)[b]
                c.e.wait_ge(sems["br_ready"], c.next("br_ready"))
                for k in range(4):
                    c.e.activation(br_hi[:, k, c0:], src[:, k, c0:], ACT.Copy).then_inc(sems["brhi_ready"], 1)
                with c.loop(f"merge{c0}", 4):
                    for j in range(2):
                        act_split(c)
                        bk = tile_wait(c)
                        c.e.wait_ge(sems["merged_ready"], c.next("merged_ready"))
                        c.e.activation(sig[:, j, c0:], ps[:, bk, c0:TOK], ACT.Sigmoid).then_inc(sems["sig_ready"], 1)
                        c.e.drain().then_inc(sems[f"free{bk}"], 1)
                        act_split(c)
                        tile_wait(c)
            c.advance("merged_ready", 2)
            c.e.wait_ge(sems["br_ready"], c.next("br_ready"))
            for k in range(KD):
                c.e.activation(h_hi[:, k, c0:], merged[:, k, c0:], ACT.Copy).then_inc(sems["mhi_ready"], 1)
            with c.loop(f"wout{c0}", 2):
                for j in range(4):
                    act_split(c)
                    c.advance("tile")

        def merge_dve(c, c0, layer, ada_from):
            for b in range(3):
                src = (attnT, gdnT, poolT)[b]
                with_ada = ada_from is not None and b == 0
                for k in range(4):
                    c.e.wait_ge(sems["brhi_ready"], c.next("brhi_ready"))
                    c.e.tensor_tensor(br_lo[:, k, c0:], src[:, k, c0:], br_hi[:, k, c0:].bitcast(F32),
                                      ALU.subtract).then_inc(sems["brlo_ready"], 1)
                if b == 0:
                    for _ in range(2):
                        c.e.drain().then_inc(sems["merged_ready"], 1)
                with c.loop(f"merge{b}{with_ada}{c0}", 4) as it:
                    for j in range(2):
                        dve_split(c)
                        c.advance("tile")
                        if with_ada and j == 0:
                            dve_ada(c, it * 2 + ada_from)
                        dve_split(c)
                        bk = tile_wait(c)
                        c.e.wait_ge(sems["sig_ready"], c.next("sig_ready"))
                        mt = merged[:, bass.ds(it * 2 + j, 1), c0:].rearrange("p a b -> p (a b)")
                        if b == 0:
                            c.e.tensor_tensor(mt, sig[:, j, c0:], ps[:, bk, c0:TOK], ALU.mult) \
                               .then_inc(sems[f"free{bk}"], 1)
                        else:
                            c.e.tensor_tensor(sig[:, j, c0:], sig[:, j, c0:], ps[:, bk, c0:TOK], ALU.mult) \
                               .then_inc(sems[f"free{bk}"], 1)
                            c.e.drain()
                            c.e.tensor_tensor(mt, mt, sig[:, j, c0:], ALU.add)
                        c.e.drain().then_inc(sems["merged_ready"], 1)
                c.e.drain().then_inc(sems["br_ready"], 1)
            for k in range(KD):
                c.e.wait_ge(sems["mhi_ready"], c.next("mhi_ready"))
                c.e.tensor_tensor(h_lo[:, k, c0:], merged[:, k, c0:], h_hi[:, k, c0:].bitcast(F32),
                                  ALU.subtract).then_inc(sems["mlo_ready"], 1)
            g0 = layer * MOD + 5 * KD
            with_ada = ada_from is not None
            with c.loop(f"wout{with_ada}{c0}", 2) as it:
                for j in range(4):
                    dve_split(c)
                    b = tile_wait(c)
                    if with_ada and j == 0:
                        dve_ada(c, it * 2 + ada_from + 8)
                    for lo, hi, s in sides[c0]:
                        xs = xT[:, bass.ds(it * 4 + j, 1), lo:hi].rearrange("p a b -> p (a b)")
                        gs = mod[:, bass.ds(it * 4 + g0 + j, 1), s:s + 1].rearrange("p a b -> p (a b)")
                        last = c.e.scalar_tensor_tensor(xs, ps[:, b, lo:hi], gs, xs, ALU.mult, ALU.add)
                    last.then_inc(sems[f"free{b}"], 1)


        SETUP = 15

        def setup_sp(c):
            def load(dst, src):
                c.e.dma_start(dst, src).then_inc(sems["dma_setup"], 16)
            load(con[:, :], a["con"])
            load(rows[:, 0:2, :], a["ctx"][0].rearrange("(t p) d -> p t d", p=P))
            load(rows[:, 2:4, :], a["x"][0].rearrange("(t p) d -> p t d", p=P))
            load(vrows[0:KD, 4, :], a["c_ctx"].rearrange("(k p) -> k p", p=P))
            load(vrows[KD:2 * KD, 4, :], a["c"][0].rearrange("(k p) -> k p", p=P))
            for v, name in ((V_N1, "norm_ffn1"), (V_NM, "norm_mix"), (V_N2, "norm_ffn2"), (V_PS, "pool_scale"),
                            (V_GN, "gdn_norm")):
                src = a[name].rearrange("l (k p) -> (l k) p", p=P)
                load(vrows[v:v + src.shape[0], 0, :], src)
            load(vrows[V_FIN:V_END, 0, :], a["final_norm"].rearrange("(k p) -> k p", p=P))
            load(vrows[0:DEPTH * CONV * 12, 1, :], a["gdn_conv"].rearrange("l t (k p) -> (l t k) p", p=P))
            load(vrows[0:MOD, 2:4, :], a["b_ada"].rearrange("l (k p) -> k l p", p=P))
            flat = a["attn_sink"].rearrange("(o l) h -> o (l h)", o=1)
            load(sink[:, :, :].rearrange("p l h -> p (l h)"), flat.to_broadcast([P, DEPTH * HEADS]))
            for t, name in ((alog, "gdn_a_log"), (dtb, "gdn_dt_bias")):
                flat = a[name].rearrange("(o l) d h -> o (l d h)", o=1)
                load(t[:, :, :, :].rearrange("p l d h -> p (l d h)"), flat.to_broadcast([P, DEPTH * 2 * GH]))

        VECS = ((4, 2 * KD), (0, V_END), (1, DEPTH * CONV * 12), (2, MOD), (3, MOD))

        def setup_pe(c):
            c.e.sem_inc(sems["tile_done"], 1)
            c.e.sem_inc(sems["ada_done"], 1)
            c.e.sem_inc(sems["ada_done"], 1)
            c.e.wait_ge(sems["dma_setup"], 16 * (SETUP + 1))
            for i, (slot, n) in enumerate(VECS):
                b = 4 + i % 2
                c.e.wait_ge(sems[f"free{b}"], c.next(f"free{b}"))
                c.e.transpose(ps[:, b, 0:n], vrows[0:n, slot, :], con[0:n, C_ID:C_ID + n]) \
                   .then_inc(sems[f"dve{b}"], 1)
            for k in range(KD):
                b = k % 4
                c.e.wait_ge(sems[f"free{b}"], c.next(f"free{b}"))
                for t in range(4):
                    last = c.e.transpose(ps[:, b, t * P:(t + 1) * P], rows[:, t, k * P:(k + 1) * P], ident)
                last.then_inc(sems[f"dve{b}"], 1)
            c.e.wait_ge(sems["c_ready"], c.next("c_ready"))
            with c.loop("ada", 8):
                pe_ada(c)

        def setup_dve(c):
            for _ in range(4):
                c.e.sem_inc(sems["lo_done"], 1)
            for _ in range(2):
                c.e.sem_inc(sems["sq_used"], 1)
            for b in range(8):
                c.e.sem_inc(sems[f"free{b}"], 1)
            c.e.memset(bias[:, 0:1], EPS)
            c.e.memset(bias[:, 1:2], math.log(GD ** -0.5))
            c.e.memset(bias[:, 2:3], 1.0)
            dst = (cT[:, :, :].rearrange("p s k -> p (s k)"), vec[:, :],
                   convw[:, :, :, :].rearrange("p l t k -> p (l t k)"), bada[:, 0:MOD], bada[:, MOD:2 * MOD])
            for i, (slot, n) in enumerate(VECS):
                b = 4 + i % 2
                c.e.wait_ge(sems[f"dve{b}"], c.next(f"dve{b}"))
                c.e.tensor_copy(dst[i], ps[:, b, 0:n]).then_inc(sems[f"free{b}"], 1)
                if i == 0:
                    c.e.drain().then_inc(sems["zero_ready"], 1)
            for k in range(KD):
                b = k % 4
                c.e.wait_ge(sems[f"dve{b}"], c.next(f"dve{b}"))
                c.e.tensor_copy(xT[:, k, :], ps[:, b, :]).then_inc(sems[f"free{b}"], 1)
            with c.loop("ada", 8) as it:
                dve_ada(c, it * 2)
            dve_split(c)
            c.e.drain()

        def result_dve(c):
            for t in range(KD):
                c.e.tensor_tensor(xT[:, t, LAT:], xT[:, t, LAT:], rstd[:, 0, LAT:], ALU.mult)
                c.e.drain()
                v = V_FIN + t
                c.e.tensor_scalar(xT[:, t, LAT:], xT[:, t, LAT:], vec[:, v:v + 1], None, ALU.mult) \
                   .then_inc(sems["fin_ready"], 1)
            for t in range(2):
                for q in range(2):
                    b = 2 * t + q
                    c.e.wait_ge(sems[f"dve{b}"], c.next(f"dve{b}"))
                    c.e.tensor_copy(rows[:, t, q * 512:(q + 1) * 512], ps[:, b, :])
                c.e.drain().then_inc(sems["o_out"], 1)

        def result_pe(c):
            for _ in range(KD):
                c.e.wait_ge(sems["fin_ready"], c.next("fin_ready"))
            for t in range(2):
                for q in range(2):
                    b = 2 * t + q
                    c.e.wait_ge(sems[f"free{b}"], c.next(f"free{b}"))
                    for k in range(4):
                        last = c.e.transpose(ps[:, b, k * P:(k + 1) * P],
                                             xT[:, 4 * q + k, LAT + t * P:LAT + (t + 1) * P], ident)
                    last.then_inc(sems[f"dve{b}"], 1)

        ADA = {(0, "ffn1"): 16, (0, "qkv"): 50, (0, "late"): 56, (0, "merge"): 60, (0, "ffn2"): 72,
               (1, "ffn1"): 106, (1, "qkv"): None, (1, "late"): 140, (1, "merge"): None, (1, "ffn2"): None}

        block = es.enter_context(nc.Block())

        @block.sync
        def _(eng):
            c = counts(eng, "sp", ())
            setup_sp(c)
            with c.loop("ada", 8) as it:
                sp_ada(c, 0, it * 2)
            for layer in range(DEPTH):
                ffn_sp(c, layer, 1, ADA[layer, "ffn1"])
                proj_sp(c, layer, ADA[layer, "qkv"])
                late_sp(c, layer, ADA[layer, "late"])
                merge_sp(c, layer, ADA[layer, "merge"])
                ffn_sp(c, layer, 2, ADA[layer, "ffn2"])
            for t in range(2):
                c.e.wait_ge(sems["o_out"], c.next("o_out"))
                c.e.dma_start(out[0, t * P:(t + 1) * P, :], rows[:, t, :]).then_inc(sems["dma_out"], 16)
            c.e.wait_ge(sems["dma_out"], 32)

        @block.gpsimd
        def _(eng):
            c = counts(eng, "pool", ())
            for layer in range(DEPTH):
                gdn_pool(c)
                c.advance("stage_free", 1)

        @block.tensor
        def _(eng):
            c = counts(eng, "pe", ("lo_done",))
            setup_pe(c)
            for layer in range(DEPTH):
                c0 = 0
                pe_norm(c, 0)
                ffn_pe(c, 0, ADA[layer, "ffn1"])
                c0 = 0 if layer < DEPTH - 1 else LAT
                pe_norm(c, 0)
                proj_pe(c, layer, c0, ADA[layer, "qkv"])
                att_pe(c, c0)
                qk_pe(c)
                gdn_pe(c)
                late_pe(c, c0)
                merge_pe(c, c0, ADA[layer, "merge"])
                pe_norm(c, c0)
                ffn_pe(c, c0, ADA[layer, "ffn2"])
            c.c0 = LAT
            pe_ssq(c)
            result_pe(c)

        @block.scalar
        def _(eng):
            c = counts(eng, "act", ())
            c.e.wait_ge(sems["zero_ready"], c.next("zero_ready"))
            c.e.activation(cT[:, :, :], cT[:, :, :], ACT.Silu).then_inc(sems["c_ready"], 1)
            act_split(c)
            for layer in range(DEPTH):
                c.layer = layer
                act_norm(c, 0)
                ffn_act(c, 0, ADA[layer, "ffn1"], False)
                c0 = 0 if layer < DEPTH - 1 else LAT
                act_norm(c, 0)
                proj_act(c, layer, c0, ADA[layer, "qkv"])
                att_act(c, c0, layer)
                qk_act(c)
                gdn_act(c)
                late_act(c, c0)
                merge_act(c, c0, ADA[layer, "merge"])
                act_norm(c, c0)
                ffn_act(c, c0, ADA[layer, "ffn2"], layer == DEPTH - 1)
            c.e.wait_ge(sems["x_ready"], c.next("x_ready"))
            for t in range(KD):
                c.e.wait_ge(sems["sq_used"], c.next("sq_used"))
                c.e.activation(sq[:, t % 2, LAT:], xT[:, t, LAT:], ACT.Square).then_inc(sems["sqn_ready"], 1)
            act_rstd(c, 4, 0, LAT, 1.0 / D, None)

        @block.vector
        def _(eng):
            c = counts(eng, "dve", ("ada_done",))
            setup_dve(c)
            for layer in range(DEPTH):
                g = layer * KD
                dve_norm(c, 0, V_N1 + g, layer, 0, 1)
                ffn_dve(c, 0, layer, 2, ADA[layer, "ffn1"], False)
                c0 = 0 if layer < DEPTH - 1 else LAT
                dve_norm(c, 0, V_NM + g, layer, 3, 4)
                proj_dve(c, layer, c0, ADA[layer, "qkv"])
                att_dve(c, c0, layer)
                qk_dve(c, layer)
                gdn_dve(c)
                late_dve(c, c0, layer, ADA[layer, "late"])
                merge_dve(c, c0, layer, ADA[layer, "merge"])
                dve_norm(c, c0, V_N2 + g, layer, 6, 7)
                ffn_dve(c, c0, layer, 8, ADA[layer, "ffn2"], layer == DEPTH - 1)
            dve_norm(c, LAT, None, None, None, None)
            result_dve(c)


def constants():
    i = np.arange(P)
    con = np.zeros((P, C_END), np.float32)

    def put(at, m):
        con[:, at:at + m.shape[1]] = m

    put(C_ID, np.eye(P))
    put(C_ONE, np.ones((P, P)))
    for d in range(2):
        keep = (i[:, None] <= i[None, :]) if d == 0 else (i[:, None] >= i[None, :])
        put(C_TRI + d * P, keep.astype(np.float32))
        put(C_NEG + d * P, np.where(keep, 0.0, NEG))
        for s in range(LEVELS):
            blk = i >> s
            m = ((blk[:, None] % 2 == 0) & (blk[None, :] == blk[:, None] + 1)).astype(np.float32)
            put(C_LEV + (d * LEVELS + s) * P, m if d == 0 else m.T)
    rot = np.zeros((P, P), np.float32)
    half = DH // 4
    for o in range(P):
        if o % (2 * half) < half:
            rot[o + half, o] = -1.0
        else:
            rot[o - half, o] = 1.0
    put(C_ROT, rot)
    for h in range(KV_HEADS):
        dup = np.zeros((P, P), np.float32)
        for o in range(P):
            dup[h * DH + o % DH, o] = 1.0
        put(C_KD + 2 * h * P, dup)
        put(C_KD + (2 * h + 1) * P, dup @ rot)
    inv = (np.float32(10000.0) ** (-np.arange(half, dtype=np.float32) / np.float32(half))).astype(np.float32)
    t = np.arange(SEG)
    for f in range(P):
        pos = (t // 64 if f % DH < DH // 2 else t % 64).astype(np.float32)
        ang = pos * inv[f % half]
        con[f, C_COS:C_COS + SEG] = np.cos(ang)
        con[f, C_SIN:C_SIN + SEG] = np.sin(ang)
    for q in range(2):
        tq = q * P + i
        put(C_MASK + q * TOK + SEG, np.where(np.abs(t[None, :] - tq[:, None]) <= WINDOW, 0.0, NEG))
    for g, w in enumerate(POOL_SIZES):
        cnt = np.clip(t + w // 2, 0, SEG) - np.clip(t - w // 2, 0, SEG)
        r = 1.0 / cnt
        con[:, C_EDGE + 16 * g:C_EDGE + 16 * g + 8] = r[:8]
        con[:, C_EDGE + 16 * g + 8:C_EDGE + 16 * g + 16] = r[-8:]
    return con


_INS = ["x", "c", "ctx", "c_ctx", "w_ada", "b_ada", "norm_ffn1", "w_ffn1_in", "w_ffn1_out", "norm_mix", "w_in",
        "attn_sink", "gdn_conv", "gdn_a_log", "gdn_dt_bias", "gdn_norm", "pool_w", "pool_scale", "w_branch_attn",
        "w_branch_gdn", "w_branch_pool", "w_out", "norm_ffn2", "w_ffn2_in", "w_ffn2_out", "final_norm"]


def kernel(**inputs):
    import concourse.bacc as bacc
    from concourse.bass_utils import run_bass_kernel_spmd as run

    nc = bacc.Bacc("TRN2", target_bir_lowering=False, num_devices=1)
    arrays, args = {}, {}
    for name in _INS + ["con"]:
        v = constants() if name == "con" else np.ascontiguousarray(inputs[name])
        arrays[f"in_{name}"] = v
        args[name] = nc.dram_tensor(f"in_{name}", v.shape, F32, kind="ExternalInput").ap()
    out = nc.dram_tensor("out_0", (1, SEG, D), F32, kind="ExternalOutput").ap()
    learned = {}
    build(nc, args, out, learned)
    if learned:
        raise ValueError("PER_TRIP = " + repr({**PER_TRIP, **learned}))
    r = run(nc, [arrays], core_ids=[0])
    return r.results[0]["out_0"]
```

```python
from contextlib import ExitStack, contextmanager
import math

import numpy as np
import concourse.bass as bass
from concourse import mybir

F32 = mybir.dt.float32
F32R = mybir.dt.float32r
ACT = mybir.ActivationFunctionType
ALU = mybir.AluOpType
AX = mybir.AxisListType

P = 128
D = 1024
KD = D // P
SEG = 256
TOK = 2 * SEG
LAT = SEG
DEPTH = 2
D_FF = 2816
HID_TILES = D_FF // P
CHUNKS = (8, 8, 6)
HEADS, KV_HEADS, DH = 8, 2, 64
WINDOW = 128
GH, GD = 4, 128
CONV = 5
PAD = CONV // 2
POOL_SIZES = (2, 4, 8, 16)
EPS = 1e-6
NEG = -1e30
LEVELS = 7
W_Q, W_K, W_V, W_QKV, W_ZG, W_AB, W_PIN, W_GL = 0, 512, 640, 768, 2304, 2816, 2832, 3344
MOD = 9 * KD
C_ID, C_ONE, C_TRI, C_NEG = 0, 128, 256, 512
C_LEV = 768
C_ROT = C_LEV + 2 * LEVELS * P
C_KD = C_ROT + P
C_COS = C_KD + 4 * P
C_SIN = C_COS + SEG
C_MASK = C_SIN + SEG
C_EDGE = C_MASK + 2 * TOK
C_END = C_EDGE + 4 * 2 * 8
V_N1, V_NM, V_N2, V_PS, V_GN, V_FIN, V_END = 0, 16, 32, 48, 56, 58, 66

PER_TRIP = {
    'act:att0': {'sc_ready': 16, 'act2': 8, 'act3': 8},
    'act:att256': {'sc_ready': 8, 'act2': 4, 'act3': 4},
    'act:ffn_in6False256': {'raw_in0': 1, 'block': 4, 'tile': 4, 'raw_in1': 1, 'hprod_ready': 2, 'raw_in2': 1, 'raw_in3': 1},
    'act:ffn_in6True0': {'raw_in1': 1, 'block': 4, 'tile': 4, 'raw_in2': 1, 'hprod_ready': 2, 'raw_in3': 1, 'raw_in0': 1},
    'act:ffn_in8False256': {'raw_in0': 1, 'block': 4, 'tile': 4, 'raw_in1': 1, 'hprod_ready': 2, 'raw_in2': 1, 'raw_in3': 1},
    'act:ffn_in8True0': {'raw_in1': 1, 'block': 4, 'tile': 4, 'raw_in2': 1, 'hprod_ready': 2, 'raw_in3': 1, 'raw_in0': 1},
    'act:ffn_out6True0': {'raw_in1': 1, 'block': 4, 'tile': 4, 'x_ready': 4, 'sq_used': 4, 'raw_in2': 1, 'raw_in3': 1, 'raw_in0': 1},
    'act:ffn_out8False256': {'raw_in0': 1, 'block': 4, 'tile': 4, 'raw_in1': 1, 'raw_in2': 1, 'raw_in3': 1},
    'act:ffn_out8True0': {'raw_in1': 1, 'block': 4, 'tile': 4, 'raw_in2': 1, 'raw_in3': 1, 'raw_in0': 1},
    'act:gdn': {'stage_free': 2, 'act0': 16, 'act3': 16, 'act_go': 4},
    'act:merge00': {'raw_in1': 1, 'block': 4, 'tile': 4, 'merged_ready': 2, 'raw_in2': 1, 'raw_in3': 1, 'raw_in0': 1},
    'act:merge0256': {'raw_in0': 1, 'block': 4, 'tile': 4, 'merged_ready': 2, 'raw_in1': 1, 'raw_in2': 1, 'raw_in3': 1},
    'act:merge10': {'raw_in1': 1, 'block': 4, 'tile': 4, 'merged_ready': 2, 'raw_in2': 1, 'raw_in3': 1, 'raw_in0': 1},
    'act:merge1256': {'raw_in0': 1, 'block': 4, 'tile': 4, 'merged_ready': 2, 'raw_in1': 1, 'raw_in2': 1, 'raw_in3': 1},
    'act:merge20': {'raw_in1': 1, 'block': 4, 'tile': 4, 'merged_ready': 2, 'raw_in2': 1, 'raw_in3': 1, 'raw_in0': 1},
    'act:merge2256': {'raw_in0': 1, 'block': 4, 'tile': 4, 'merged_ready': 2, 'raw_in1': 1, 'raw_in2': 1, 'raw_in3': 1},
    'act:qkv0': {'raw_in1': 1, 'block': 4, 'tile': 4, 'pad_used': 4, 'raw_in2': 1, 'raw_in3': 1, 'raw_in0': 1},
    'act:qkv256': {'raw_in0': 1, 'block': 4, 'tile': 4, 'pad_used': 4, 'raw_in1': 1, 'raw_in2': 1, 'raw_in3': 1},
    'act:wout0': {'raw_in1': 1, 'block': 4, 'tile': 4, 'x_ready': 4, 'sq_used': 4, 'raw_in2': 1, 'raw_in3': 1, 'raw_in0': 1},
    'act:wout256': {'raw_in0': 1, 'block': 4, 'tile': 4, 'x_ready': 4, 'sq_used': 4, 'raw_in1': 1, 'raw_in2': 1, 'raw_in3': 1},
    'dve:ada': {'ada_row': 2, 'ada_done': 1},
    'dve:att0': {'dve4': 2, 'dve0': 8, 'dve1': 8, 'exp_ready': 16, 'dve5': 8, 'dve6': 8},
    'dve:att256': {'dve4': 2, 'dve0': 4, 'dve1': 4, 'exp_ready': 8, 'dve5': 4, 'dve6': 4},
    'dve:ffn_in6False256': {'hi_done': 4, 'block': 4, 'tile': 4, 'sil_ready': 2, 'hidhi_ready': 2},
    'dve:ffn_in6True0': {'hi_done': 4, 'block': 4, 'ada_row': 2, 'tile': 4, 'sil_ready': 2, 'hidhi_ready': 2, 'ada_done': 1},
    'dve:ffn_in8False256': {'hi_done': 4, 'block': 4, 'tile': 4, 'sil_ready': 2, 'hidhi_ready': 2},
    'dve:ffn_in8True0': {'hi_done': 4, 'block': 4, 'ada_row': 2, 'tile': 4, 'sil_ready': 2, 'hidhi_ready': 2, 'ada_done': 1},
    'dve:ffn_out6True0': {'hi_done': 4, 'block': 4, 'ada_row': 2, 'tile': 4, 'sqn_ready': 4, 'ada_done': 1},
    'dve:ffn_out8False256': {'hi_done': 4, 'block': 4, 'tile': 4},
    'dve:ffn_out8True0': {'hi_done': 4, 'block': 4, 'ada_row': 2, 'tile': 4, 'ada_done': 1},
    'dve:gdn': {'dve1': 18, 'dve4': 18, 'e_ready': 6, 'dve2': 16, 'dve0': 4, 'dve5': 16, 'dve3': 4},
    'dve:merge0False256': {'hi_done': 4, 'block': 4, 'tile': 4, 'sig_ready': 2},
    'dve:merge0True0': {'hi_done': 4, 'block': 4, 'tile': 4, 'ada_row': 2, 'sig_ready': 2, 'ada_done': 1},
    'dve:merge1False0': {'hi_done': 4, 'block': 4, 'tile': 4, 'sig_ready': 2},
    'dve:merge1False256': {'hi_done': 4, 'block': 4, 'tile': 4, 'sig_ready': 2},
    'dve:merge2False0': {'hi_done': 4, 'block': 4, 'tile': 4, 'sig_ready': 2},
    'dve:merge2False256': {'hi_done': 4, 'block': 4, 'tile': 4, 'sig_ready': 2},
    'dve:qkv0True': {'hi_done': 4, 'block': 4, 'tile': 4, 'ada_row': 2, 'pad_ready': 4, 'ada_done': 1},
    'dve:qkv256False': {'hi_done': 4, 'block': 4, 'tile': 4, 'pad_ready': 4},
    'dve:woutFalse256': {'hi_done': 4, 'block': 4, 'tile': 4, 'sqn_ready': 4},
    'dve:woutTrue0': {'hi_done': 4, 'block': 4, 'ada_row': 2, 'tile': 4, 'sqn_ready': 4, 'ada_done': 1},
    'pe:ada': {'free7': 1, 'ada_in0': 1, 'ada_in1': 1, 'arow_ready': 1},
    'pe:att0': {'free4': 2, 'qs_ready': 2, 'free0': 8, 'free1': 8, 'p_ready': 16, 'free2': 8, 'free3': 8, 'pT_ready': 16, 'free5': 8, 'free6': 8},
    'pe:att256': {'free4': 2, 'qs_ready': 2, 'free0': 4, 'free1': 4, 'p_ready': 8, 'free2': 4, 'free3': 4, 'pT_ready': 8, 'free5': 4, 'free6': 4},
    'pe:ffn_in6FalseFalse': {'lo_done': 4, 'free2': 1, 'block': 4, 'free3': 1, 'free0': 1, 'free1': 1},
    'pe:ffn_in6FalseTrue': {'free7': 1, 'ada_in0': 1, 'ada_in1': 1, 'lo_done': 4, 'free3': 1, 'block': 4, 'free0': 1, 'arow_ready': 1, 'free1': 1, 'free2': 1},
    'pe:ffn_in8FalseFalse': {'lo_done': 4, 'free2': 1, 'block': 4, 'free3': 1, 'free0': 1, 'free1': 1},
    'pe:ffn_in8FalseTrue': {'free7': 1, 'ada_in0': 1, 'ada_in1': 1, 'lo_done': 4, 'free3': 1, 'block': 4, 'free0': 1, 'arow_ready': 1, 'free1': 1, 'free2': 1},
    'pe:ffn_in8TrueFalse': {'lo_done': 4, 'free2': 1, 'block': 4, 'free3': 1, 'free0': 1, 'free1': 1},
    'pe:ffn_in8TrueTrue': {'free7': 1, 'ada_in0': 1, 'ada_in1': 1, 'lo_done': 4, 'free3': 1, 'block': 4, 'free0': 1, 'arow_ready': 1, 'free1': 1, 'free2': 1},
    'pe:gdn': {'pe_go': 40, 'free1': 18, 'free4': 18, 'staged': 4, 'free0': 20, 'free3': 20, 'free2': 16, 'q_staged': 4, 'free5': 16, 'p_copied': 24, 'u_ready': 24},
    'pe:mergeFalse': {'lo_done': 4, 'free2': 1, 'block': 4, 'free3': 1, 'free0': 1, 'free1': 1},
    'pe:mergeTrue': {'free7': 1, 'ada_in0': 1, 'ada_in1': 1, 'lo_done': 4, 'free3': 1, 'block': 4, 'free0': 1, 'arow_ready': 1, 'free1': 1, 'free2': 1},
    'pe:qkvFalse': {'lo_done': 4, 'free2': 1, 'block': 4, 'free3': 1, 'free0': 1, 'free1': 1},
    'pe:qkvTrue': {'free7': 1, 'ada_in0': 1, 'ada_in1': 1, 'lo_done': 4, 'free3': 1, 'block': 4, 'free0': 1, 'arow_ready': 1, 'free1': 1, 'free2': 1},
    'pool:gdn': {'stage_free': 2},
    'sp:ada': {'ada_row': 2},
    'sp:ffn_in6False': {'tile_done': 4, 'block': 4},
    'sp:ffn_in6True': {'ada_row': 2, 'tile_done': 4, 'block': 4},
    'sp:ffn_in8False': {'tile_done': 4, 'block': 4},
    'sp:ffn_in8True': {'ada_row': 2, 'tile_done': 4, 'block': 4},
    'sp:ffn_out6False': {'tile_done': 4, 'block': 4},
    'sp:ffn_out6True': {'ada_row': 2, 'tile_done': 4, 'block': 4},
    'sp:ffn_out8False': {'tile_done': 4, 'block': 4},
    'sp:ffn_out8True': {'ada_row': 2, 'tile_done': 4, 'block': 4},
    'sp:mergeFalse': {'tile_done': 4, 'block': 4},
    'sp:mergeTrue': {'ada_row': 2, 'tile_done': 4, 'block': 4},
    'sp:qkvFalse': {'tile_done': 4, 'block': 4},
    'sp:qkvTrue': {'ada_row': 2, 'tile_done': 4, 'block': 4},
    'sp:woutFalse': {'tile_done': 4, 'block': 4},
    'sp:woutTrue': {'ada_row': 2, 'tile_done': 4, 'block': 4},
}


class Counts:

    def __init__(self, eng, sems, who, start, learned):
        self.e, self.sems, self.who, self.learned = eng, sems, who, learned
        self.base = dict(start)
        self.body, self.it, self.per = {}, None, {}

    def advance(self, name, k=1):
        if self.it is None:
            self.base[name] = self.base.get(name, 0) + k
        else:
            self.body[name] = self.body.get(name, 0) + k

    def static(self, name):
        return self.base.get(name, 0) + self.body.get(name, 0)

    def value(self, name, scale=1, plus=0):
        v = (self.static(name) + plus) * scale
        if self.it is not None and self.per.get(name, 0):
            v = self.it * (self.per[name] * scale) + v
        return v

    def next(self, name):
        self.advance(name)
        return self.value(name, 16 if name.startswith(("raw_in", "ada_in", "dma_")) else 1)

    @contextmanager
    def loop(self, name, trips):
        key = f"{self.who}:{name}"
        with self.e.Fori(0, trips) as it:
            self.it, self.per, self.body = it, PER_TRIP.get(key, {}), {}
            yield it
        if self.body != self.per:
            self.learned[key] = dict(self.body)
        for k, v in self.body.items():
            self.base[k] = self.base.get(k, 0) + v * trips
        self.body, self.it, self.per = {}, None, {}


def build(nc, a, out, learned):
    es = ExitStack()
    sems = {}

    def sb(name, shape, dt=F32, stack=es):
        return stack.enter_context(nc.sbuf_tensor(name, shape, dt))

    with es:
        xT = sb("xT", [P, KD, TOK])
        h_hi = sb("h_hi", [P, KD, TOK], F32R)
        h_lo = sb("h_lo", [P, KD, TOK], F32R)
        raw, w_lo = [], []
        for i in range(4):
            with ExitStack() as m:
                raw.append(sb(f"raw{i}", [P, 1024], F32, m))
            w_lo.append(sb(f"w_lo{i}", [P, 1024], F32R))
        w_hi = sb("w_hi", [P, 4, 1024], F32R)
        ada_w = sb("ada_w", [P, 2, 1024])
        arow = sb("arow", [2, 2 * P])
        mod = sb("mod", [P, DEPTH * MOD, 2])
        bada = sb("bada", [P, DEPTH * MOD])
        con = sb("con", [P, C_END])
        vec = sb("vec", [P, V_END])
        convw = sb("convw", [P, DEPTH, CONV, 12])
        cT = sb("cT", [P, 2, KD])
        sink = sb("sink", [P, DEPTH, HEADS])
        alog = sb("alog", [P, DEPTH, 2, GH])
        dtb = sb("dtb", [P, DEPTH, 2, GH])
        bias = sb("bias", [P, 4])
        sq = sb("sq", [P, 2, TOK])
        acc = sb("acc", [P, TOK])
        rstd = sb("rstd", [P, 2, TOK])
        hx = sb("hx", [P, 2, TOK])
        am = sb("am", [P, KD, 2])
        gate = sb("gate", [P, KD, 2])
        gates = sb("gates", [P, 2, 4, GH])
        beta = sb("beta", [P, 2, 4, GH])
        gcn = sb("gcn", [P, 2, 4, GH])
        negeg = sb("negeg", [P, 2, 4, GH])
        gtot = sb("gtot", [P, 2, 4, GH])
        dec = sb("dec", [P, 2, 4, GH])
        gtmp = sb("gtmp", [P, 3, 2, 4, GH])
        stat = sb("stat", [P, 4, 6])
        ps = es.enter_context(nc.psum_tensor("ps", [P, 8, 512], F32))

        with ExitStack() as m:
            attnT = sb("attnT", [P, 4, TOK], F32, m)
            gdnT = sb("gdnT", [P, GH, TOK], F32, m)
            with ExitStack() as m2:
                qkvT = sb("qkvT", [P, 12, TOK], F32, m2)
                with ExitStack() as m3:
                    G = sb("G", [P, 2, 9, 4, P], F32, m3)
                    state = sb("state", [P, 2, GH, P], F32, m3)
                with ExitStack() as m3:
                    qksq = sb("qksq", [P, 8, TOK], F32, m3)
                    qkrs = sb("qkrs", [P, 8, TOK], F32, m3)
                with ExitStack() as m3:
                    pad = sb("pad", [P, 2, 2, SEG + 2 * PAD], F32, m3)
                    kv = sb("kv", [P, 2, TOK], F32, m3)
                    kd = sb("kd", [P, KV_HEADS, TOK], F32, m3)
                    vnat = sb("vnat", [P, 4, P], F32, m3)
                    qs = sb("qs", [P, 2, TOK], F32, m3)
                    sc = sb("sc", [P, 3, TOK], F32, m3)
                    pT = sb("pT", [P, 2, 4, P], F32, m3)
                    rtmp = sb("rtmp", [P, 2, SEG], F32, m3)
            with ExitStack() as m2:
                poolT = sb("poolT", [P, 4, TOK], F32, m2)
                br_hi = sb("br_hi", [P, 4, TOK], F32R, m2)
                br_lo = sb("br_lo", [P, 4, TOK], F32R, m2)
                merged = sb("merged", [P, KD, TOK], F32, m2)
                sig = sb("sig", [P, 2, TOK], F32, m2)
                ppad = sb("ppad", [P, 2, 2, SEG + 16], F32, m2)
                pool_s = sb("pool_s", [P, 2, 2, SEG + 16], F32, m2)
                pw = sb("pw", [P, 4, P], F32, m2)
        with ExitStack() as m:
            hid_hi = sb("hid_hi", [P, 8, TOK], F32R, m)
            hid_lo = sb("hid_lo", [P, 8, TOK], F32R, m)
            sil = sb("sil", [P, 2, TOK], F32, m)
            hprod = sb("hprod", [P, 2, TOK], F32, m)
        with ExitStack() as m:
            rows = sb("rows", [P, 4, D], F32, m)
            vrows = sb("vrows", [P, 6, P], F32, m)

        KTS, QS, VN, EE, NT, TT, UU, PP, NM = range(9)

        names = (["hi_done", "lo_done", "tile_done", "ada_row", "arow_ready", "ada_done", "dma_setup", "dma_out", "dma_pw"]
                 + [f"raw_in{i}" for i in range(4)] + [f"ada_in{i}" for i in range(2)]
                 + [f"free{b}" for b in range(8)] + [f"act{b}" for b in range(8)] + [f"dve{b}" for b in range(8)]
                 + ["x_ready", "sq_ready", "sq_used", "ssq_ready", "rstd_ready", "hx_ready", "hhi_ready",
                    "h_ready", "sil_ready", "hprod_ready", "hidhi_ready", "hid_ready", "c_ready", "zero_ready",
                    "kv_ready", "kd_ready", "qraw_ready", "qs_ready", "pad_ready", "pad_used", "conv_ready",
                    "silu_ready", "qkn_ready", "sc_ready", "exp_ready", "p_ready", "pT_ready", "act_go", "pe_go", "p_copied", "e_ready", "gdn_over", "att_over", "q_staged", "u_ready", "sqn_ready",
                    "stage_free", "staged", "ab_ready", "abexp_ready", "g_ready", "gcx_ready",
                    "o_ready", "osq_ready", "z_ready", "br_ready", "brhi_ready", "brlo_ready", "sig_ready", "pin_ready",
                    "pool_ready", "merged_ready", "mhi_ready", "mlo_ready", "fin_ready", "o_out", "unused"])
        for n in names:
            sems[n] = es.enter_context(nc.semaphore(n))
        CREDIT = {"tile_done": 4, "ada_row": 2, "sq_used": 2, }

        def counts(eng, who, credited):
            return Counts(eng, sems, who, {n: CREDIT[n] for n in credited}, learned)

        ident = con[:, C_ID:C_ID + P]
        ones = con[:, C_ONE:C_ONE + P]

        def tri(d):
            return con[:, C_TRI + d * P:C_TRI + (d + 1) * P]

        def negm(d):
            return con[:, C_NEG + d * P:C_NEG + (d + 1) * P]

        def lev(d, s):
            o = C_LEV + (d * LEVELS + s) * P
            return con[:, o:o + P]

        def heads(ap):
            return ap.rearrange("p (a b) -> p a b", a=1).to_broadcast([P, GH, P])

        def bank4(b):
            return ps[:, b, :].rearrange("p (h c) -> p h c", h=4)

        sides = {0: ((0, SEG, 0), (SEG, TOK, 1)), LAT: ((SEG, TOK, 1),)}

        def sp_block(c, src, k0, nk, col, width=P):
            s = c.static("block") % 4
            c.e.wait_ge(sems["tile_done"], c.next("tile_done"))
            c.e.sem_inc(sems["unused"], 1)
            dst = raw[s][:, 0:nk * width].rearrange("p (k c) -> p k c", k=nk)
            c.e.dma_start(dst, src[k0 * P:(k0 + nk) * P, bass.ds(col, width)]
                          .rearrange("(k p) c -> p k c", p=P)).then_inc(sems[f"raw_in{s}"], 16)
            c.advance("block")

        def sp_ada(c, layer, tile):
            for i in range(2):
                c.e.wait_ge(sems["ada_row"], c.next("ada_row"))
                c.e.sem_inc(sems["unused"], 1)
                c.e.dma_start(ada_w[:, i, :].rearrange("p (k c) -> p k c", k=KD),
                              a["w_ada"][layer, :, bass.ds((tile + i) * P, P)]
                              .rearrange("(k p) c -> p k c", p=P)).then_inc(sems[f"ada_in{i}"], 16)

        def act_split(c, nk=KD):
            n = c.static("block") % 4
            c.e.wait_ge(sems[f"raw_in{n}"], c.next(f"raw_in{n}"))
            c.e.activation(w_hi[:, n, 0:nk * P], raw[n][:, 0:nk * P], ACT.Copy).then_inc(sems["hi_done"], 1)
            c.advance("block")

        def dve_split(c, nk=KD):
            n = c.static("block") % 4
            c.e.wait_ge(sems["hi_done"], c.next("hi_done"))
            c.e.tensor_tensor(w_lo[n][:, 0:nk * P], raw[n][:, 0:nk * P], w_hi[:, n, 0:nk * P].bitcast(F32),
                              ALU.subtract).then_inc(sems["lo_done"], 1)
            c.advance("block")

        def pe_tile(c, rhs_hi, rhs_lo, nk, c0, skip=0, each=None):
            n = c.static("block")
            b = s = n % 4
            c.e.wait_ge(sems["lo_done"], c.next("lo_done"))
            c.e.wait_ge(sems[f"free{b}"], c.next(f"free{b}"))
            for k in range(nk):
                w = slice((skip + k) * P, (skip + k + 1) * P)
                if each is not None:
                    c.e.wait_ge(sems[each], c.next(each))
                hi, lo = w_hi[:, s, w], w_lo[s][:, w]
                o = ps[:, b, c0:TOK]
                c.e.matmul(o, hi, rhs_hi[:, k, c0:TOK], start=(k == 0), stop=False)
                c.e.matmul(o, hi, rhs_lo[:, k, c0:TOK], start=False, stop=False)
                last = c.e.matmul(o, lo, rhs_hi[:, k, c0:TOK], start=False, stop=(k == nk - 1))
            last.then_inc(sems["tile_done"], 1)
            c.advance("block")

        def pe_ada(c):
            c.e.wait_ge(sems["free7"], c.next("free7"))
            for i in range(2):
                c.e.wait_ge(sems[f"ada_in{i}"], c.next(f"ada_in{i}"))
                for k in range(KD):
                    last = c.e.matmul(ps[0:2, 7, i * P:(i + 1) * P], cT[:, :, k], ada_w[:, i, k * P:(k + 1) * P],
                                      start=(k == 0), stop=(k == KD - 1))
                last.then_inc(sems["ada_row"], 1)

        def pe_ada_turn(c):
            c.e.wait_ge(sems["arow_ready"], c.next("arow_ready"))
            for i in range(2):
                last = c.e.matmul(ps[:, 7, 256 + 2 * i:258 + 2 * i], arow[0:2, i * P:(i + 1) * P],
                                  con[0:2, C_ID:C_ID + 2], start=True, stop=True)
            last.then_inc(sems["ada_done"], 1)

        def dve_ada_row(c):
            c.e.wait_ge(sems["ada_row"], c.next("ada_row"))
            c.e.wait_ge(sems["ada_row"], c.next("ada_row"))
            c.e.tensor_copy(arow[0:2, :], ps[0:2, 7, 0:256]).then_inc(sems["arow_ready"], 1)

        def dve_ada(c, tile):
            c.e.wait_ge(sems["ada_done"], c.next("ada_done"))
            c.e.tensor_tensor(mod[:, bass.ds(tile, 2), :], ps[:, 7, 256:260].rearrange("p (t s) -> p t s", t=2),
                              bada[:, bass.ds(tile, 2)].rearrange("p (t s) -> p t s", s=1).to_broadcast([P, 2, 2]),
                              ALU.add).then_inc(sems["free7"], 1)

        def tile_wait(c):
            n = c.static("tile")
            c.advance("tile")
            c.e.wait_ge(sems["tile_done"], c.value("tile", plus=CREDIT["tile_done"]))
            return n % 4

        def act_square(c, slot, xt, c0):
            c.e.wait_ge(sems["x_ready"], c.next("x_ready"))
            c.e.wait_ge(sems["sq_used"], c.next("sq_used"))
            c.e.activation(sq[:, slot:slot + 1, c0:], xT[:, xt, c0:], ACT.Square).then_inc(sems["sqn_ready"], 1)

        def act_norm(c, c0, layer, shift):
            act_rstd(c, 4, 0, c0, 1.0 / D, None)
            for t in range(KD):
                c.e.wait_ge(sems["hx_ready"], c.next("hx_ready"))
                b0 = layer * MOD + shift * KD + t
                for lo, hi, s in sides[c0]:
                    c.e.activation(hx[:, t % 2, lo:hi], hx[:, t % 2, lo:hi], ACT.Identity,
                                   bias=mod[:, b0, s:s + 1], scale=am[:, t, s:s + 1])
                c.e.drain()
                c.e.activation(h_hi[:, t, c0:], hx[:, t % 2, c0:], ACT.Copy).then_inc(sems["hhi_ready"], 1)

        def act_rstd(c, b, r, c0, scale, q_bias):
            c.e.wait_ge(sems[f"act{b}"], c.next(f"act{b}"))
            c.e.activation(rstd[:, r, c0:], ps[:, b, c0:TOK], ACT.Ln, bias=bias[:, 0:1], scale=scale) \
               .then_inc(sems[f"free{b}"], 1)
            c.e.drain()
            c.e.activation(rstd[:, r, c0:], rstd[:, r, c0:], ACT.Exp, bias=q_bias if q_bias is not None else 0.0,
                           scale=-0.5).then_inc(sems["rstd_ready"], 1)

        def pe_ssq(c):
            c.e.wait_ge(sems["ssq_ready"], c.next("ssq_ready"))
            c.e.wait_ge(sems["free4"], c.next("free4"))
            c.e.matmul(ps[:, 4, c.c0:TOK], ones, acc[:, c.c0:], start=True, stop=True).then_inc(sems["act4"], 1)

        def dve_sum_start(c, c0):
            c.e.memset(acc[:, c0:], 0.0)

        def dve_sum_square(c, slot, c0):
            c.e.drain().then_inc(sems["x_ready"], 1)
            c.e.wait_ge(sems["sqn_ready"], c.next("sqn_ready"))
            c.e.tensor_tensor(acc[:, c0:], acc[:, c0:], sq[:, slot, c0:], ALU.add).then_inc(sems["sq_used"], 1)

        def dve_norm(c, c0, gain, layer, scale):
            c.e.drain().then_inc(sems["ssq_ready"], 1)
            if layer is None:
                c.e.wait_ge(sems["rstd_ready"], c.next("rstd_ready"))
                return
            s0 = layer * MOD + scale * KD
            c.e.scalar_tensor_tensor(am[:, :, :], mod[:, s0:s0 + KD, :], 1.0,
                                     vec[:, gain:gain + KD].rearrange("p (t s) -> p t s", s=1)
                                     .to_broadcast([P, KD, 2]), ALU.add, ALU.mult)
            c.e.drain()
            c.e.wait_ge(sems["rstd_ready"], c.next("rstd_ready"))
            for t in range(KD + 1):
                if t < KD:
                    c.e.tensor_tensor(hx[:, t % 2, c0:], xT[:, t, c0:], rstd[:, 0, c0:], ALU.mult) \
                       .then_inc(sems["hx_ready"], 1)
                if t > 0:
                    c.e.wait_ge(sems["hhi_ready"], c.next("hhi_ready"))
                    c.e.tensor_tensor(h_lo[:, t - 1, c0:], hx[:, (t - 1) % 2, c0:],
                                      h_hi[:, t - 1, c0:].bitcast(F32), ALU.subtract).then_inc(sems["h_ready"], 1)
                    c.e.drain()

        def pe_norm(c, c0):
            c.c0 = c0
            pe_ssq(c)

        def ffn_plan(which):
            first = 0
            for i, n in enumerate(CHUNKS):
                yield i, first, n
                first += n

        def ffn_sp(c, layer, which, ada_from):
            wi, wo = a[f"w_ffn{which}_in"][layer], a[f"w_ffn{which}_out"][layer]
            ada = ada_from
            for i, first, n in ffn_plan(which):
                done = 1 if i == 0 and layer == 0 and which == 1 else 0
                if done:
                    sp_ada(c, 0, ada)
                with c.loop(f"ffn_in{n}{ada is not None}", n // 2 - done) as it:
                    if ada is not None:
                        sp_ada(c, ada // MOD, it * 2 + ada % MOD + 2 * done)
                    for j in range(2):
                        sp_block(c, wi, 0, KD, it * 256 + (first + 2 * done + j) * P)
                        sp_block(c, wi, 0, KD, it * 256 + D_FF + (first + 2 * done + j) * P)
                if ada is not None:
                    ada += n
                with c.loop(f"ffn_out{n}{ada is not None}", 2) as it:
                    if ada is not None:
                        sp_ada(c, ada // MOD, it * 2 + ada % MOD)
                    for j in range(4):
                        sp_block(c, wo, first + n - KD, KD, it * 512 + j * P)
                if ada is not None:
                    ada += 4

        def ffn_pe(c, c0, ada_from):
            ada = ada_from is not None
            for i, first, n in ffn_plan(0):

                def trip(each):
                    if ada:
                        pe_ada(c)
                    for j in range(4):
                        if ada and j == 2:
                            pe_ada_turn(c)
                        pe_tile(c, h_hi, h_lo, KD, c0, each=each if j == 0 else None)

                if i == 0:
                    trip("h_ready")
                with c.loop(f"ffn_in{n}{i == 0}{ada}", n // 2 - (i == 0)):
                    trip(None)
                for half in range(2):
                    if ada:
                        pe_ada(c)
                    for j in range(4):
                        if ada and j == 2:
                            pe_ada_turn(c)
                        pe_tile(c, hid_hi, hid_lo, n, c0, KD - n, "hid_ready" if half + j == 0 else None)

        def ffn_act(c, c0, ada_from, final):
            ada = ada_from is not None
            for i, first, n in ffn_plan(0):
                with c.loop(f"ffn_in{n}{ada}{c0}", n // 2) as it:
                    for j in range(2):
                        act_split(c)
                        b = tile_wait(c)
                        c.e.activation(sil[:, j, c0:], ps[:, b, c0:TOK], ACT.Silu).then_inc(sems["sil_ready"], 1)
                        act_split(c)
                        tile_wait(c)
                        c.e.wait_ge(sems["hprod_ready"], c.next("hprod_ready"))
                        c.e.activation(hid_hi[:, bass.ds(it * 2 + j, 1), c0:], hprod[:, j:j + 1, c0:], ACT.Copy) \
                           .then_inc(sems["hidhi_ready"], 1)
                if final and i == len(CHUNKS) - 1:
                    for j in range(8):
                        if j < 6:
                            act_split(c)
                        c.advance("tile")
                        act_square(c, j % 2, slice(j, j + 1), c0)
                else:
                    with c.loop(f"ffn_out{n}{ada}{c0}", 2) as it:
                        for j in range(4):
                            act_split(c)
                            c.advance("tile")
                            if i == len(CHUNKS) - 1:
                                act_square(c, j % 2, bass.ds(it * 4 + j, 1), c0)

        def ffn_dve(c, c0, layer, gate_at, ada_from, final):
            ada = ada_from
            for i, first, n in ffn_plan(0):
                with c.loop(f"ffn_in{n}{ada is not None}{c0}", n // 2) as it:
                    for j in range(2):
                        dve_split(c)
                        if ada is not None and j == 0:
                            dve_ada_row(c)
                        elif ada is not None:
                            dve_ada(c, it * 2 + ada)
                        bg = tile_wait(c)
                        dve_split(c)
                        bu = tile_wait(c)
                        c.e.wait_ge(sems["sil_ready"], c.next("sil_ready"))
                        c.e.tensor_tensor(hprod[:, j, c0:], sil[:, j, c0:], ps[:, bu, c0:TOK], ALU.mult) \
                           .then_inc(sems["hprod_ready"], 1)
                        c.e.drain().then_inc(sems[f"free{bg}"], 1)
                        c.e.drain().then_inc(sems[f"free{bu}"], 1)
                        c.e.wait_ge(sems["hidhi_ready"], c.next("hidhi_ready"))
                        c.e.tensor_tensor(hid_lo[:, bass.ds(it * 2 + j, 1), c0:], hprod[:, j:j + 1, c0:],
                                          hid_hi[:, bass.ds(it * 2 + j, 1), c0:].bitcast(F32),
                                          ALU.subtract).then_inc(sems["hid_ready"], 1)
                if ada is not None:
                    ada += n
                if i == 0:
                    g0 = layer * MOD + gate_at * KD
                    c.e.drain()
                    c.e.tensor_scalar(gate[:, :, :], mod[:, g0:g0 + KD, :], 0.5, None, ALU.mult)
                    c.e.drain()

                def out_tile(f, slot, split, row=False, columns=None):
                    if split:
                        dve_split(c)
                    if row:
                        dve_ada_row(c)
                    if columns is not None:
                        dve_ada(c, columns)
                    b = tile_wait(c)
                    for lo, hi, s in sides[c0]:
                        xs = xT[:, bass.ds(f, 1), lo:hi].rearrange("p a b -> p (a b)")
                        gs = gate[:, bass.ds(f, 1), s:s + 1].rearrange("p a b -> p (a b)")
                        last = c.e.scalar_tensor_tensor(xs, ps[:, b, lo:hi], gs, xs, ALU.mult, ALU.add)
                    last.then_inc(sems[f"free{b}"], 1)
                    if i == len(CHUNKS) - 1:
                        dve_sum_square(c, slot, c0)

                if i == len(CHUNKS) - 1:
                    dve_sum_start(c, c0)
                if final and i == len(CHUNKS) - 1:
                    for j in range(8):
                        out_tile(j, j % 2, j < 6)
                else:
                    with c.loop(f"ffn_out{n}{ada is not None}{c0}", 2) as it:
                        for j in range(4):
                            out_tile(it * 4 + j, j % 2, True, ada is not None and j == 0,
                                     it * 2 + ada if ada is not None and j == 2 else None)
                    if ada is not None:
                        ada += 4

        def proj_sp(c, layer, ada_from):
            w = a["w_in"][layer]
            for j in range(4):
                sp_block(c, w, 0, KD, W_Q + j * P)
            sp_block(c, w, 0, KD, W_K)
            sp_block(c, w, 0, KD, W_V)
            sp_block(c, w, 0, KD, W_AB, 16)
            with c.loop(f"qkv{ada_from is not None}", 3) as it:
                if ada_from is not None:
                    sp_ada(c, ada_from // MOD, it * 2 + ada_from % MOD)
                for j in range(4):
                    sp_block(c, w, 0, KD, it * 512 + W_QKV + j * P)

        def proj_pe(c, layer, c0, ada_from):
            for j in range(4):
                pe_tile(c, h_hi, h_lo, KD, c0, each="h_ready" if j == 0 else None)
            pe_tile(c, h_hi, h_lo, KD, 0)
            pe_tile(c, h_hi, h_lo, KD, 0)
            n = c.static("block")
            b = s = n % 4
            c.e.wait_ge(sems["lo_done"], c.next("lo_done"))
            c.e.wait_ge(sems[f"free{b}"], c.next(f"free{b}"))
            for t in range(4):
                cols = slice(t * P, (t + 1) * P)
                o = ps[:, b, t * 16:(t + 1) * 16]
                for k in range(KD):
                    hi, lo = w_hi[:, s, k * 16:(k + 1) * 16], w_lo[s][:, k * 16:(k + 1) * 16]
                    c.e.matmul(o, h_hi[:, k, cols], hi, start=(k == 0), stop=False)
                    c.e.matmul(o, h_hi[:, k, cols], lo, start=False, stop=False)
                    last = c.e.matmul(o, h_lo[:, k, cols], hi, start=False, stop=(k == KD - 1))
            last.then_inc(sems["tile_done"], 1)
            c.advance("block")
            with c.loop(f"qkv{ada_from is not None}", 3):
                if ada_from is not None:
                    pe_ada(c)
                for j in range(4):
                    if ada_from is not None and j == 2:
                        pe_ada_turn(c)
                    pe_tile(c, h_hi, h_lo, KD, 0)
            c.e.wait_ge(sems["kv_ready"], c.next("kv_ready"))
            for h in range(KV_HEADS):
                for r in range(2):
                    b = 4 + r
                    c.e.wait_ge(sems[f"free{b}"], c.next(f"free{b}"))
                    o = C_KD + (2 * h + r) * P
                    c.e.matmul(ps[:, b, (LAT if r else 0):TOK], con[:, o:o + P], kv[:, 0, (LAT if r else 0):],
                               start=True, stop=True).then_inc(sems[f"dve{b}"], 1)
            c.e.wait_ge(sems["free6"], c.next("free6"))
            for t in range(4):
                last = c.e.transpose(ps[:, 6, t * P:(t + 1) * P], kv[:, 1, t * P:(t + 1) * P], ident)
            last.then_inc(sems["act6"], 1)

        def proj_act(c, layer, c0, ada_from):
            for j in range(4):
                act_split(c)
                b = tile_wait(c)
                c.e.activation(attnT[:, j, c0:], ps[:, b, c0:TOK], ACT.Copy).then_inc(sems[f"free{b}"], 1)
            c.e.drain().then_inc(sems["qraw_ready"], 1)
            for j in range(2):
                act_split(c, 1 if j == 0 else KD)
                b = tile_wait(c)
                c.e.activation(kv[:, j, :], ps[:, b, :], ACT.Copy).then_inc(sems[f"free{b}"], 1)
            c.e.drain().then_inc(sems["kv_ready"], 1)
            act_split(c)
            c.advance("tile")
            with c.loop(f"qkv{c0}", 3) as it:
                for j in range(4):
                    act_split(c)
                    b = tile_wait(c)
                    c.e.wait_ge(sems["pad_used"], c.next("pad_used"))
                    c.e.activation(pad[:, j % 2, :, PAD:PAD + SEG],
                                   ps[:, b, :].rearrange("p (s t) -> p s t", s=2), ACT.Copy) \
                       .then_inc(sems["pad_ready"], 1)
                    c.e.drain().then_inc(sems[f"free{b}"], 1)
            c.advance("pad_used", 2)
            c.e.wait_ge(sems["act6"], c.next("act6"))
            c.e.activation(vnat[:, :, :], bank4(6), ACT.Copy).then_inc(sems["free6"], 1)
            c.e.drain().then_inc(sems["kd_ready"], 1)

        def proj_dve(c, layer, c0, ada_from):
            c.e.memset(pad[:, :, :, 0:PAD], 0.0)
            c.e.memset(pad[:, :, :, PAD + SEG:], 0.0)
            for _ in range(2):
                c.e.drain().then_inc(sems["pad_used"], 1)
            for j in range(6):
                dve_split(c, 1 if j == 4 else KD)
                c.advance("tile")
            dve_split(c)
            b = tile_wait(c)
            ab = ps[:, b, 0:64].rearrange("p (t d h) -> p d t h", t=4, h=GH)
            for d in range(2):
                c.e.tensor_tensor(gtmp[:, 0, d], ab[:, d],
                                  dtb[:, layer, d:d + 1, :].to_broadcast([P, 4, GH]), ALU.add)
                c.e.tensor_scalar(beta[:, d], ab[:, 2 + d], -1.0, None, ALU.mult)
            c.e.drain().then_inc(sems[f"free{b}"], 1)
            c.e.tensor_scalar(gtmp[:, 2], gtmp[:, 0], -1.0, None, ALU.mult)
            c.e.drain()
            c.e.tensor_tensor(gtmp[:, 1], gtmp[:, 2], gtmp[:, 0], ALU.min)
            c.e.drain().then_inc(sems["ab_ready"], 1)
            with c.loop(f"qkv{c0}{ada_from is not None}", 3) as it:
                for j in range(4):
                    dve_split(c)
                    c.advance("tile")
                    if ada_from is not None and j == 0:
                        dve_ada_row(c)
                    if ada_from is not None and j == 2:
                        dve_ada(c, it * 2 + ada_from)
                    c.e.wait_ge(sems["pad_ready"], c.next("pad_ready"))
                    o = qkvT[:, bass.ds(it * 4 + j, 1), :].rearrange("p a (s t) -> p (a s) t", s=2)

                    def cw(tap):
                        return convw[:, layer, tap, bass.ds(it * 4 + j, 1)]

                    c.e.tensor_scalar(o, pad[:, j % 2, :, 0:SEG], cw(0), None, ALU.mult)
                    for tap in range(1, CONV):
                        c.e.drain()
                        last = c.e.scalar_tensor_tensor(o, pad[:, j % 2, :, tap:tap + SEG], cw(tap), o,
                                                        ALU.mult, ALU.add)
                    last.then_inc(sems["pad_used"], 1)
            c.e.drain().then_inc(sems["conv_ready"], 1)
            for h in range(KV_HEADS):
                c.e.wait_ge(sems["dve4"], c.next("dve4"))
                c.e.tensor_copy(kd[:, h, 0:LAT], ps[:, 4, 0:LAT])
                c.e.tensor_tensor(rtmp[:, 0, :], ps[:, 4, LAT:TOK], con[:, C_COS:C_COS + SEG], ALU.mult) \
                   .then_inc(sems["free4"], 1)
                c.e.wait_ge(sems["dve5"], c.next("dve5"))
                c.e.tensor_tensor(rtmp[:, 1, :], ps[:, 5, LAT:TOK], con[:, C_SIN:C_SIN + SEG], ALU.mult) \
                   .then_inc(sems["free5"], 1)
                c.e.drain()
                c.e.tensor_tensor(kd[:, h, LAT:TOK], rtmp[:, 0, :], rtmp[:, 1, :], ALU.add)
                c.e.drain()
            c.e.wait_ge(sems["kd_ready"], c.next("kd_ready"))

        def att_items(c0):
            return [(kvh, hh, qt) for kvh in range(2) for hh in range(2) for qt in range(c0 // P, 4)]

        def att_pe(c, c0):
            items = att_items(c0)
            n = len(items)
            with c.loop(f"att{c0}", 2) as it:
                for kvh in range(2):
                    c.e.wait_ge(sems["free4"], c.next("free4"))
                    c.e.matmul(ps[:, 4, LAT:TOK], con[:, C_ROT:C_ROT + P],
                               attnT[:, bass.ds(it + 2 * kvh, 1), LAT:], start=True, stop=True) \
                       .then_inc(sems["dve4"], 1)
                for k in range(n + 3):
                    if k < n:
                        kvh, hh, qt = items[k]
                        if k == 0 or items[k - 1][0] != kvh:
                            c.e.wait_ge(sems["qs_ready"], c.next("qs_ready"))
                        b = k % 2
                        c.e.wait_ge(sems[f"free{b}"], c.next(f"free{b}"))
                        p = slice(64 * hh, 64 * hh + 64)
                        nk = TOK if qt >= 2 else SEG
                        c.e.matmul(ps[:, b, 0:nk], qs[p, kvh, qt * P:(qt + 1) * P], kd[p, kvh, 0:nk],
                                   start=True, stop=True).then_inc(sems[f"dve{b}"], 1)
                    if 0 <= k - 2 < n:
                        i = k - 2
                        b = 2 + i % 2
                        c.e.wait_ge(sems["p_ready"], c.next("p_ready"))
                        c.e.wait_ge(sems[f"free{b}"], c.next(f"free{b}"))
                        for kb in range(4 if items[i][2] >= 2 else 2):
                            last = c.e.transpose(ps[:, b, kb * P:(kb + 1) * P], sc[:, i % 3, kb * P:(kb + 1) * P],
                                                 ident)
                        last.then_inc(sems[f"act{b}"], 1)
                    if 0 <= k - 3 < n:
                        i = k - 3
                        kvh, hh, qt = items[i]
                        b = 5 + i % 2
                        c.e.wait_ge(sems["pT_ready"], c.next("pT_ready"))
                        c.e.wait_ge(sems[f"free{b}"], c.next(f"free{b}"))
                        nb = 4 if qt >= 2 else 2
                        for kb in range(nb):
                            last = c.e.matmul(ps[64 * hh:64 * hh + 64, b, 0:P], vnat[:, kb, 64 * kvh:64 * kvh + 64],
                                              pT[:, i % 2, kb, :], start=(kb == 0), stop=(kb == nb - 1))
                        last.then_inc(sems[f"dve{b}"], 1)

        def att_dve(c, c0, layer):
            items = att_items(c0)
            n = len(items)
            c.e.wait_ge(sems["qraw_ready"], c.next("qraw_ready"))
            with c.loop(f"att{c0}", 2) as it:
                for kvh in range(2):
                    q = attnT[:, bass.ds(it + 2 * kvh, 1), :].rearrange("p a b -> p (a b)")
                    if c0 == 0:
                        c.e.tensor_copy(qs[:, kvh, 0:LAT], attnT[:, bass.ds(it + 2 * kvh, 1), 0:LAT]
                                        .rearrange("p a b -> p (a b)"))
                    c.e.tensor_tensor(rtmp[:, 0, :], attnT[:, bass.ds(it + 2 * kvh, 1), LAT:]
                                      .rearrange("p a b -> p (a b)"), con[:, C_COS:C_COS + SEG], ALU.mult)
                    c.e.wait_ge(sems["dve4"], c.next("dve4"))
                    c.e.tensor_tensor(rtmp[:, 1, :], ps[:, 4, LAT:TOK], con[:, C_SIN:C_SIN + SEG], ALU.mult) \
                       .then_inc(sems["free4"], 1)
                    c.e.drain()
                    c.e.tensor_tensor(qs[:, kvh, LAT:], rtmp[:, 0, :], rtmp[:, 1, :], ALU.add)
                    c.e.drain().then_inc(sems["qs_ready"], 1)
                for k in range(n + 3):
                    if k < n:
                        kvh, hh, qt = items[k]
                        b, r = k % 2, k % 3
                        nk = TOK if qt >= 2 else SEG
                        hc = bass.ds(it * 2 + 4 * kvh + hh, 1)
                        c.e.wait_ge(sems[f"dve{b}"], c.next(f"dve{b}"))
                        if qt >= 2:
                            mk = con[:, C_MASK + (qt - 2) * TOK:C_MASK + (qt - 1) * TOK]
                            c.e.scalar_tensor_tensor(sc[:, r, :], ps[:, b, :], DH ** -0.5, mk, ALU.mult, ALU.add) \
                               .then_inc(sems[f"free{b}"], 1)
                        else:
                            c.e.tensor_scalar(sc[:, r, 0:nk], ps[:, b, 0:nk], DH ** -0.5, None, ALU.mult) \
                               .then_inc(sems[f"free{b}"], 1)
                        c.e.drain()
                        c.e.tensor_reduce(stat[:, k % 4, 0:1], sc[:, r, 0:nk], AX.X, ALU.max)
                        c.e.drain()
                        c.e.tensor_scalar(stat[:, k % 4, 1:2], stat[:, k % 4, 0:1], sink[:, layer, hc], -1.0,
                                          ALU.max, ALU.mult).then_inc(sems["sc_ready"], 1)
                    if 0 <= k - 1 < n:
                        i = k - 1
                        nk = TOK if items[i][2] >= 2 else SEG
                        st = stat[:, i % 4, :]
                        c.e.wait_ge(sems["exp_ready"], c.next("exp_ready"))
                        c.e.tensor_tensor(st[:, 4:5], st[:, 2:3], st[:, 3:4], ALU.add)
                        c.e.drain()
                        c.e.reciprocal(st[:, 5:6], st[:, 4:5])
                        c.e.drain()
                        c.e.tensor_scalar(sc[:, i % 3, 0:nk], sc[:, i % 3, 0:nk], st[:, 5:6], None, ALU.mult) \
                           .then_inc(sems["p_ready"], 1)
                    if 0 <= k - 3 < n:
                        i = k - 3
                        kvh, hh, qt = items[i]
                        b = 5 + i % 2
                        p = slice(64 * hh, 64 * hh + 64)
                        c.e.wait_ge(sems[f"dve{b}"], c.next(f"dve{b}"))
                        c.e.tensor_scalar(attnT[p, bass.ds(it + 2 * kvh, 1), qt * P:(qt + 1) * P],
                                          ps[p, b, 0:P].rearrange("p (a b) -> p a b", a=1), 1.0, None, ALU.mult) \
                           .then_inc(sems[f"free{b}"], 1)
                c.e.drain()

        def att_act(c, c0, layer):
            items = att_items(c0)
            n = len(items)
            with c.loop(f"att{c0}", 2) as it:
                for k in range(n + 2):
                    if k < n:
                        kvh, hh, qt = items[k]
                        nk = TOK if qt >= 2 else SEG
                        st = stat[:, k % 4, :]
                        hc = bass.ds(it * 2 + 4 * kvh + hh, 1)
                        c.e.wait_ge(sems["sc_ready"], c.next("sc_ready"))
                        c.e.activation(sc[:, k % 3, 0:nk], sc[:, k % 3, 0:nk], ACT.Exp, bias=st[:, 1:2],
                                       accum_out=st[:, 2:3])
                        c.e.activation(st[:, 3:4], sink[:, layer, hc], ACT.Exp, bias=st[:, 1:2])
                        c.e.drain().then_inc(sems["exp_ready"], 1)
                    if 0 <= k - 2 < n:
                        i = k - 2
                        b = 2 + i % 2
                        nb = 4 if items[i][2] >= 2 else 2
                        c.e.wait_ge(sems[f"act{b}"], c.next(f"act{b}"))
                        c.e.activation(pT[:, i % 2, 0:nb, :], bank4(b)[:, 0:nb, :], ACT.Copy) \
                           .then_inc(sems["pT_ready"], 1)
                        c.e.drain().then_inc(sems[f"free{b}"], 1)

        def qk_act(c):
            c.e.wait_ge(sems["conv_ready"], c.next("conv_ready"))
            for t in range(3):
                c.e.activation(qkvT[:, 4 * t:4 * t + 4, :], qkvT[:, 4 * t:4 * t + 4, :], ACT.Silu)
                c.e.drain()
            c.e.drain().then_inc(sems["silu_ready"], 1)
            c.e.wait_ge(sems["att_over"], c.next("att_over"))
            for t in range(2 * GH):
                c.e.activation(qksq[:, t, :], qkvT[:, t, :], ACT.Square).then_inc(sems["sq_ready"], 1)
            c.e.wait_ge(sems["ab_ready"], c.next("ab_ready"))
            c.e.activation(gtmp[:, 1], gtmp[:, 1], ACT.Exp)
            c.e.activation(beta[:, :], beta[:, :], ACT.Exp)
            c.e.activation(gtmp[:, 2, :, 0, :], alog[:, c.layer], ACT.Exp)
            c.e.drain()
            c.e.activation(gtmp[:, 1], gtmp[:, 1], ACT.Ln, bias=bias[:, 2:3])
            c.e.drain().then_inc(sems["abexp_ready"], 1)
            for t in range(2 * GH):
                b = 4 + t % 2
                c.e.wait_ge(sems[f"act{b}"], c.next(f"act{b}"))
                c.e.activation(qkrs[:, t, :], ps[:, b, :], ACT.Ln, bias=bias[:, 0:1]).then_inc(sems[f"free{b}"], 1)
            c.e.drain()
            for t in range(2 * GH):
                c.e.activation(qkrs[:, t, :], qkrs[:, t, :], ACT.Exp, bias=bias[:, 1:2] if t < GH else 0.0,
                               scale=-0.5).then_inc(sems["rstd_ready"], 1)
            c.e.wait_ge(sems["act6"], c.next("act6"))
            c.e.activation(gcn[:, :, :, :], ps[:, 6, 0:32].rearrange("p (d t h) -> p d t h", d=2, h=GH), ACT.Copy)
            c.e.activation(negeg[:, :, :, :], ps[:, 6, 0:32].rearrange("p (d t h) -> p d t h", d=2, h=GH), ACT.Exp)
            c.e.activation(gtot[:, :, :, :], ps[:, 6, 32:64].rearrange("p (d t h) -> p d t h", d=2, h=GH), ACT.Exp)
            c.e.drain().then_inc(sems["gcx_ready"], 1)
            c.e.wait_ge(sems["act_go"], c.next("act_go"))
            c.e.activation(dec[:, :, :, :], dec[:, :, :, :], ACT.Exp)
            c.e.drain().then_inc(sems["gcx_ready"], 1)

        def qk_pe(c):
            for t in range(2 * GH):
                b = 4 + t % 2
                c.e.wait_ge(sems["sq_ready"], c.next("sq_ready"))
                c.e.wait_ge(sems[f"free{b}"], c.next(f"free{b}"))
                c.e.matmul(ps[:, b, :], ones, qksq[:, t, :], start=True, stop=True).then_inc(sems[f"act{b}"], 1)
            c.e.wait_ge(sems["g_ready"], c.next("g_ready"))
            c.e.wait_ge(sems["free6"], c.next("free6"))
            for d in range(2):
                c.e.matmul(ps[:, 6, 16 * d:16 * d + 16], tri(d), gates[:, d], start=True, stop=True)
            c.e.matmul(ps[:, 6, 32:64], ones, gates[:, :, :, :].rearrange("p d t h -> p (d t h)"),
                       start=True, stop=True).then_inc(sems["act6"], 1)

        def qk_dve(c, layer):
            c.e.drain().then_inc(sems["att_over"], 1)
            c.e.wait_ge(sems["silu_ready"], c.next("silu_ready"))
            c.e.wait_ge(sems["abexp_ready"], c.next("abexp_ready"))
            c.e.scalar_tensor_tensor(gtmp[:, 0], gtmp[:, 0], 0.0, gtmp[:, 1], ALU.max, ALU.add)
            c.e.tensor_scalar(beta[:, :], beta[:, :], 1.0, None, ALU.add)
            c.e.drain()
            for d in range(2):
                c.e.scalar_tensor_tensor(gates[:, d], gtmp[:, 0, d], -1.0,
                                         gtmp[:, 2, d, 0:1, :].to_broadcast([P, 4, GH]), ALU.mult, ALU.mult)
            c.e.reciprocal(beta[:, :], beta[:, :])
            c.e.drain().then_inc(sems["g_ready"], 1)
            c.e.memset(state[:, :, :, :], 0.0)
            for t in range(2 * GH):
                c.e.wait_ge(sems["rstd_ready"], c.next("rstd_ready"))
                c.e.tensor_tensor(qkvT[:, t, :], qkvT[:, t, :], qkrs[:, t, :], ALU.mult)
            c.e.wait_ge(sems["gcx_ready"], c.next("gcx_ready"))
            c.e.tensor_tensor(dec[:, :, :, :], ps[:, 6, 32:64].rearrange("p (d t h) -> p d t h", d=2, h=GH),
                              gcn[:, :, :, :], ALU.subtract)
            c.e.tensor_scalar(negeg[:, :, :, :], negeg[:, :, :, :], -1.0, None, ALU.mult)
            c.e.drain().then_inc(sems["free6"], 1)
            c.e.drain().then_inc(sems["act_go"], 1)
            c.e.wait_ge(sems["gcx_ready"], c.next("gcx_ready"))
            c.e.drain().then_inc(sems["stage_free"], 1)

        def steps():
            return [(step, d) for step in range(2) for d in range(2)]

        def tile_of(it, step, d):
            return it * 2 + (step if d == 0 else 1 - step)

        def gdn_pool(c):
            with c.loop("gdn", 2) as it:
                for step in range(2):
                    c.e.wait_ge(sems["stage_free"], c.next("stage_free"))
                    c.e.sem_inc(sems["unused"], 1)
                    for d in range(2):
                        cols = bass.ds(tile_of(it, step, d) * P, P)
                        c.e.tensor_copy(G[:, d, QS], qkvT[:, 0:4, cols]).then_inc(sems["q_staged"], 1)

        def mm4(c, b, f, to="dve"):
            c.e.wait_ge(sems[f"free{b}"], c.next(f"free{b}"))
            for h in range(GH):
                last = f(h, ps[:, b, h * P:(h + 1) * P])
            last.then_inc(sems[f"{to}{b}"], 1)

        def gdn_pe(c):
            mm = c.e.matmul
            with c.loop("gdn", 2):
                for step in range(2):
                    for d in range(2):
                        g = G[:, d]
                        c.e.wait_ge(sems["pe_go"], c.next("pe_go"))
                        b = 3 * d + 1
                        c.e.wait_ge(sems[f"free{b}"], c.next(f"free{b}"))
                        mm(ps[:, b, :], ones, g[:, PP].rearrange("p h c -> p (h c)"), start=True, stop=True) \
                            .then_inc(sems[f"dve{b}"], 1)
                    for d in range(2):
                        g = G[:, d]
                        c.e.wait_ge(sems["staged"], c.next("staged"))
                        mm4(c, 3 * d, lambda h, o: c.e.transpose(o, g[:, UU, h], ident), "act")
                    for d in range(2):
                        g = G[:, d]
                        mm4(c, 3 * d + 2, lambda h, o: mm(o, g[:, KTS, h], g[:, KTS, h], start=True, stop=True))
                        c.e.wait_ge(sems["q_staged"], c.next("q_staged"))
                        mm4(c, 3 * d, lambda h, o: mm(o, g[:, KTS, h], g[:, QS, h], start=True, stop=True))
                    for d in range(2):
                        g = G[:, d]
                        c.e.wait_ge(sems["pe_go"], c.next("pe_go"))
                        mm4(c, 3 * d + 1, lambda h, o: c.e.transpose(o, g[:, UU, h], ident))
                    for s in range(1, LEVELS):
                        for d in range(2):
                            g = G[:, d]
                            c.e.wait_ge(sems["pe_go"], c.next("pe_go"))
                            mm4(c, 3 * d, lambda h, o: mm(o, g[:, NM, h], g[:, TT, h], start=True, stop=True), "act")
                        for d in range(2):
                            g = G[:, d]
                            c.e.wait_ge(sems["p_copied"], c.next("p_copied"))
                            if s > 1:
                                c.e.wait_ge(sems["u_ready"], c.next("u_ready"))
                            if s < LEVELS - 1:
                                mm4(c, 3 * d + 1, lambda h, o: mm(o, g[:, UU, h], g[:, PP, h], start=True, stop=True))
                            mm4(c, 3 * d + 2, lambda h, o: mm(o, g[:, PP, h], g[:, UU, h], start=True, stop=True))
                    for d in range(2):
                        g = G[:, d]
                        c.e.wait_ge(sems["u_ready"], c.next("u_ready"))
                        mm4(c, 3 * d, lambda h, o: c.e.transpose(o, g[:, KTS, h], ident), "act")
                        mm4(c, 3 * d + 1, lambda h, o: mm(o, g[:, KTS, h], state[:, d, h], start=True, stop=True))
                    for d in range(2):
                        g = G[:, d]
                        c.e.wait_ge(sems["pe_go"], c.next("pe_go"))
                        mm4(c, 3 * d + 2, lambda h, o: mm(o, g[:, UU, h], g[:, VN, h], start=True, stop=True))
                    for d in range(2):
                        g = G[:, d]
                        c.e.wait_ge(sems["pe_go"], c.next("pe_go"))
                        b = 3 * d
                        c.e.wait_ge(sems[f"free{b}"], c.next(f"free{b}"))
                        for h in range(GH):
                            o = ps[:, b, h * P:(h + 1) * P]
                            mm(o, state[:, d, h], g[:, QS, h], start=True, stop=False)
                            last = mm(o, g[:, TT, h], g[:, EE, h], start=False, stop=True)
                        last.then_inc(sems[f"dve{b}"], 1)
                        mm4(c, b + 1, lambda h, o: mm(o, g[:, NM, h], g[:, PP, h], start=True, stop=True))

        def gdn_act(c):
            with c.loop("gdn", 2) as it:
                for step in range(2):
                    c.e.wait_ge(sems["stage_free"], c.next("stage_free"))
                    c.e.sem_inc(sems["unused"], 1)
                    for d in range(2):
                        cols = bass.ds(tile_of(it, step, d) * P, P)
                        c.e.activation(G[:, d, UU], qkvT[:, 8:12, cols], ACT.Copy)
                        c.e.activation(G[:, d, KTS], qkvT[:, 4:8, cols], ACT.Copy)
                        c.e.drain().then_inc(sems["staged"], 1)
                    for d in range(2):
                        c.e.wait_ge(sems[f"act{3 * d}"], c.next(f"act{3 * d}"))
                        c.e.activation(G[:, d, VN], bank4(3 * d), ACT.Copy).then_inc(sems[f"free{3 * d}"], 1)
                    for d in range(2):
                        c.e.wait_ge(sems["act_go"], c.next("act_go"))
                        c.e.activation(G[:, d, EE], G[:, d, EE], ACT.Exp)
                        c.e.activation(G[:, d, TT], bank4(3 * d + 1), ACT.Exp).then_inc(sems[f"free{3 * d + 1}"], 1)
                        c.e.drain().then_inc(sems["e_ready"], 1)
                    for s in range(1, LEVELS):
                        for d in range(2):
                            c.e.wait_ge(sems[f"act{3 * d}"], c.next(f"act{3 * d}"))
                            c.e.activation(G[:, d, PP], bank4(3 * d), ACT.Copy).then_inc(sems["p_copied"], 1)
                            c.e.drain().then_inc(sems[f"free{3 * d}"], 1)
                    for d in range(2):
                        c.e.wait_ge(sems[f"act{3 * d}"], c.next(f"act{3 * d}"))
                        c.e.activation(G[:, d, NM], bank4(3 * d), ACT.Copy).then_inc(sems[f"free{3 * d}"], 1)
                    c.e.drain().then_inc(sems["e_ready"], 1)

        def gdn_dve(c):
            with c.loop("gdn", 2) as it:
                for step in range(2):
                    gt = [bass.ds(tile_of(it, step, d), 1) for d in range(2)]

                    def col(buf, d, h):
                        return buf[:, d, gt[d], h:h + 1].rearrange("p a b -> p (a b)")

                    for d in range(2):
                        g = G[:, d]
                        c.e.tensor_tensor(g[:, PP], heads(tri(d)),
                                          gates[:, d, gt[d], :].rearrange("p a h -> p h a").to_broadcast([P, GH, P]),
                                          ALU.mult).then_inc(sems["pe_go"], 1)
                    for d in range(2):
                        g = G[:, d]
                        b = 3 * d + 1
                        c.e.wait_ge(sems[f"dve{b}"], c.next(f"dve{b}"))
                        for h in range(GH):
                            last = c.e.scalar_tensor_tensor(g[:, EE, h], ps[:, b, h * P:(h + 1) * P], col(gcn, d, h),
                                                            negm(d), ALU.subtract, ALU.add)
                        last.then_inc(sems["act_go"], 1)
                    for d in range(2):
                        g = G[:, d]
                        c.e.wait_ge(sems["e_ready"], c.next("e_ready"))
                        b = 3 * d + 2
                        c.e.wait_ge(sems[f"dve{b}"], c.next(f"dve{b}"))
                        for h in range(GH):
                            last = c.e.scalar_tensor_tensor(g[:, NT, h], ps[:, b, h * P:(h + 1) * P],
                                                            col(beta, d, h), g[:, EE, h], ALU.mult, ALU.mult)
                        last.then_inc(sems[f"free{b}"], 1)
                        c.e.drain()
                        c.e.wait_ge(sems[f"dve{3 * d}"], c.next(f"dve{3 * d}"))
                        c.e.tensor_tensor(g[:, EE], bank4(3 * d), g[:, EE], ALU.mult).then_inc(sems[f"free{3 * d}"], 1)
                        c.e.tensor_tensor(g[:, QS], g[:, QS], g[:, TT], ALU.mult)
                        c.e.drain()
                        c.e.tensor_tensor(g[:, UU], g[:, NT], heads(lev(d, 0)), ALU.mult)
                        c.e.drain()
                        c.e.scalar_tensor_tensor(g[:, UU], g[:, UU], -1.0, heads(ident), ALU.mult, ALU.add) \
                           .then_inc(sems["pe_go"], 1)
                    for d in range(2):
                        g = G[:, d]
                        c.e.tensor_tensor(g[:, NM], g[:, NT], heads(lev(d, 1)), ALU.mult)
                        c.e.wait_ge(sems[f"dve{3 * d + 1}"], c.next(f"dve{3 * d + 1}"))
                        c.e.tensor_copy(g[:, TT], bank4(3 * d + 1)).then_inc(sems[f"free{3 * d + 1}"], 1)
                        c.e.drain().then_inc(sems["pe_go"], 1)
                    for s in range(1, LEVELS):
                        if s < LEVELS - 1:
                            for d in range(2):
                                g = G[:, d]
                                b = 3 * d + 1
                                c.e.wait_ge(sems[f"dve{b}"], c.next(f"dve{b}"))
                                if d == 0:
                                    for dn in range(2):
                                        c.e.tensor_tensor(G[:, dn, NM], G[:, dn, NT], heads(lev(dn, s + 1)), ALU.mult)
                                c.e.tensor_tensor(g[:, TT], g[:, TT], bank4(b), ALU.subtract) \
                                   .then_inc(sems[f"free{b}"], 1)
                                c.e.drain().then_inc(sems["pe_go"], 1)
                        for d in range(2):
                            g = G[:, d]
                            b = 3 * d + 2
                            c.e.wait_ge(sems[f"dve{b}"], c.next(f"dve{b}"))
                            c.e.tensor_tensor(g[:, UU], g[:, UU], bank4(b), ALU.subtract).then_inc(sems[f"free{b}"], 1)
                            c.e.drain().then_inc(sems["u_ready"], 1)
                    for d in range(2):
                        g = G[:, d]
                        b = 3 * d + 1
                        c.e.wait_ge(sems[f"dve{b}"], c.next(f"dve{b}"))
                        for h in range(GH):
                            last = c.e.scalar_tensor_tensor(g[:, VN, h], ps[:, b, h * P:(h + 1) * P],
                                                            col(negeg, d, h), g[:, VN, h], ALU.mult, ALU.add)
                        c.e.drain().then_inc(sems[f"free{b}"], 1)
                        c.e.drain().then_inc(sems["pe_go"], 1)
                    c.e.wait_ge(sems["e_ready"], c.next("e_ready"))
                    for d in range(2):
                        g = G[:, d]
                        b = 3 * d + 2
                        c.e.wait_ge(sems[f"dve{b}"], c.next(f"dve{b}"))
                        for h in range(GH):
                            c.e.tensor_scalar(g[:, TT, h], ps[:, b, h * P:(h + 1) * P], col(beta, d, h), None,
                                              ALU.mult)
                            c.e.tensor_scalar(g[:, PP, h], ps[:, b, h * P:(h + 1) * P], col(beta, d, h),
                                              col(dec, d, h), ALU.mult, ALU.mult)
                        c.e.drain().then_inc(sems[f"free{b}"], 1)
                        c.e.drain().then_inc(sems["pe_go"], 1)
                    for d in range(2):
                        g = G[:, d]
                        b = 3 * d
                        o = gdnT[:, :, bass.ds(tile_of(it, step, d) * P, P)]
                        c.e.wait_ge(sems[f"dve{b}"], c.next(f"dve{b}"))
                        if step == 0:
                            c.e.tensor_scalar(o, bank4(b), 1.0, None, ALU.mult).then_inc(sems[f"free{b}"], 1)
                        else:
                            c.e.tensor_tensor(o, o, bank4(b), ALU.add).then_inc(sems[f"free{b}"], 1)
                        b = 3 * d + 1
                        c.e.wait_ge(sems[f"dve{b}"], c.next(f"dve{b}"))
                        for h in range(GH):
                            last = c.e.scalar_tensor_tensor(state[:, d, h], state[:, d, h], col(gtot, d, h),
                                                            ps[:, b, h * P:(h + 1) * P], ALU.mult, ALU.add)
                        last.then_inc(sems[f"free{b}"], 1)
                    c.e.drain().then_inc(sems["stage_free"], 1)
            c.e.drain().then_inc(sems["gdn_over"], 1)

        def late_sp(c, layer, ada_from):
            w = a["w_in"][layer]
            for part, w0 in enumerate((W_ZG, W_PIN)):
                sp_ada(c, (ada_from + 2 * part) // MOD, (ada_from + 2 * part) % MOD)
                for j in range(4):
                    sp_block(c, w, 0, KD, w0 + j * P)
            c.e.wait_ge(sems["z_ready"], c.next("z_ready"))
            c.e.dma_start(pw[:, :, :], a["pool_w"][layer].rearrange("g c d -> c g d")) \
               .then_inc(sems["dma_pw"], 16)

        def late_pe(c, c0):
            pe_ada(c)
            for j in range(4):
                if j == 2:
                    pe_ada_turn(c)
                pe_tile(c, h_hi, h_lo, KD, c0)
            def sum_square(h):
                c.e.wait_ge(sems["sq_ready"], c.next("sq_ready"))
                b = 4 + h % 2
                c.e.wait_ge(sems[f"free{b}"], c.next(f"free{b}"))
                c.e.matmul(ps[:, b, c0:TOK], ones, sq[:, h % 2, c0:], start=True, stop=True) \
                   .then_inc(sems[f"act{b}"], 1)

            pe_ada(c)
            for j in range(4):
                if j == 2:
                    pe_ada_turn(c)
                pe_tile(c, h_hi, h_lo, KD, c0)
                if j > 0:
                    sum_square(j - 1)
            sum_square(GH - 1)
            c.e.wait_ge(sems["dma_pw"], c.next("dma_pw"))
            for g in range(4):
                c.e.wait_ge(sems["pin_ready"], c.next("pin_ready"))
                b = 6
                c.e.wait_ge(sems[f"free{b}"], c.next(f"free{b}"))
                c.e.matmul(ps[:, b, c0:TOK], pw[:, g, :], poolT[:, g, c0:], start=True, stop=True) \
                   .then_inc(sems[f"dve{b}"], 1)

        def late_act(c, c0):
            for j in range(4):
                act_split(c)
                b = tile_wait(c)
                if j == 0:
                    c.e.wait_ge(sems["gdn_over"], c.next("gdn_over"))
                c.e.activation(merged[:, j, c0:], ps[:, b, c0:TOK], ACT.Silu).then_inc(sems[f"free{b}"], 1)
            c.e.drain().then_inc(sems["z_ready"], 1)
            c.e.drain().then_inc(sems["o_ready"], 1)
            for j in range(4):
                act_split(c, 4 if j == 3 else KD)
                b = tile_wait(c)
                c.e.wait_ge(sems["pad_used"], c.next("pad_used"))
                n = 2 if c0 == 0 else 1
                c.e.activation(ppad[:, j % 2, 2 - n:2, 8:8 + SEG],
                               ps[:, b, c0:TOK].rearrange("p (s t) -> p s t", s=n), ACT.Copy) \
                   .then_inc(sems["pad_ready"], 1)
                c.e.drain().then_inc(sems[f"free{b}"], 1)
                c.e.wait_ge(sems["sq_used"], c.next("sq_used"))
                c.e.activation(sq[:, j % 2, c0:], gdnT[:, j, c0:], ACT.Square).then_inc(sems["sq_ready"], 1)
                if j > 0:
                    act_rstd(c, 4 + (j - 1) % 2, (j - 1) % 2, c0, 1.0 / GD, None)
            c.advance("pad_used", 2)
            act_rstd(c, 4 + (GH - 1) % 2, (GH - 1) % 2, c0, 1.0 / GD, None)

        def late_dve(c, c0, layer, ada_from):
            s0 = 0 if c0 == 0 else 1

            def gated(h):
                c.e.wait_ge(sems["rstd_ready"], c.next("rstd_ready"))
                c.e.tensor_tensor(gdnT[:, h, c0:], gdnT[:, h, c0:], rstd[:, h % 2, c0:], ALU.mult)
                c.e.drain()
                c.e.scalar_tensor_tensor(gdnT[:, h, c0:], gdnT[:, h, c0:],
                                         vec[:, V_GN + layer:V_GN + layer + 1], merged[:, h, c0:],
                                         ALU.mult, ALU.mult)
                c.e.drain().then_inc(sems["sq_used"], 1)

            for part in range(2):
                for j in range(4):
                    dve_split(c, 4 if part == 1 and j == 3 else KD)
                    c.advance("tile")
                    if j == 0:
                        dve_ada_row(c)
                    if j == 2:
                        dve_ada(c, ada_from + 2 * part)
                    if part == 0:
                        continue
                    if j == 0:
                        c.e.wait_ge(sems["o_ready"], c.next("o_ready"))
                        c.e.memset(ppad[:, :, :, 0:8], 0.0)
                        c.e.memset(ppad[:, :, :, 8 + SEG:], 0.0)
                        c.e.drain().then_inc(sems["pad_used"], 1)
                        c.e.drain().then_inc(sems["pad_used"], 1)
                    c.e.wait_ge(sems["pad_ready"], c.next("pad_ready"))
                    src = ppad[:, j % 2, s0:2, :]
                    w, n = 1, SEG + 16
                    cur = src
                    for lv in range(j + 1):
                        n -= w
                        nxt = pool_s[:, lv % 2, s0:2, 0:n]
                        c.e.tensor_tensor(nxt, cur[:, :, 0:n], cur[:, :, w:w + n], ALU.add)
                        c.e.drain()
                        cur = nxt
                        w *= 2
                    o = poolT[:, j, c0:].rearrange("p (s t) -> p s t", t=SEG)
                    off = 8 - w // 2
                    c.e.tensor_scalar(o, cur[:, :, off:off + SEG], 1.0 / w, None, ALU.mult)
                    c.e.drain()
                    for e, at in ((0, 0), (1, SEG - 8)):
                        ed = con[:, C_EDGE + (j * 2 + e) * 8:C_EDGE + (j * 2 + e + 1) * 8]
                        c.e.tensor_tensor(o[:, :, at:at + 8], cur[:, :, off + at:off + at + 8],
                                          ed.rearrange("p (s t) -> p s t", s=1).to_broadcast([P, 2 - s0, 8]), ALU.mult)
                    c.e.drain()
                    c.e.tensor_tensor(o, o, src[:, :, 8:8 + SEG], ALU.subtract)
                    c.e.drain().then_inc(sems["pin_ready"], 1)
                    c.e.drain().then_inc(sems["pad_used"], 1)
                    if j > 0:
                        gated(j - 1)
            gated(GH - 1)
            for g in range(4):
                c.e.wait_ge(sems["dve6"], c.next("dve6"))
                v = V_PS + layer * 4 + g
                c.e.tensor_scalar(poolT[:, g, c0:], ps[:, 6, c0:TOK], vec[:, v:v + 1], None, ALU.mult) \
                   .then_inc(sems["free6"], 1)
            c.e.drain().then_inc(sems["br_ready"], 1)

        def merge_sp(c, layer, ada_from):
            w = a["w_in"][layer]
            ada = ada_from
            for b, name in enumerate(("w_branch_attn", "w_branch_gdn", "w_branch_pool")):
                with_ada = ada_from is not None and b == 0
                with c.loop(f"merge{with_ada}", 4) as it:
                    if with_ada:
                        sp_ada(c, ada // MOD, it * 2 + ada % MOD)
                    for j in range(2):
                        sp_block(c, w, 0, KD, it * 256 + W_GL + b * D + j * P)
                        sp_block(c, a[name][layer], 0, 4, it * 256 + j * P)
            with_ada = ada_from is not None
            with c.loop(f"wout{with_ada}", 2) as it:
                if with_ada:
                    sp_ada(c, (ada + 8) // MOD, it * 2 + (ada + 8) % MOD)
                for j in range(4):
                    sp_block(c, a["w_out"][layer], 0, KD, it * 512 + j * P)

        def merge_pe(c, c0, ada_from):
            for b in range(3):
                with_ada = ada_from is not None and b == 0

                def trip(each):
                    if with_ada:
                        pe_ada(c)
                    for j in range(2):
                        if with_ada and j == 1:
                            pe_ada_turn(c)
                        pe_tile(c, h_hi, h_lo, KD, c0)
                        pe_tile(c, br_hi, br_lo, 4, c0, each=each if j == 0 else None)

                trip("brlo_ready")
                with c.loop(f"merge{with_ada}", 3):
                    trip(None)
            with_ada = ada_from is not None
            for half in range(2):
                if with_ada:
                    pe_ada(c)
                for j in range(4):
                    if with_ada and j == 2:
                        pe_ada_turn(c)
                    pe_tile(c, h_hi, h_lo, KD, c0, each="mlo_ready" if half + j == 0 else None)

        def merge_act(c, c0, ada_from):
            for b in range(3):
                src = (attnT, gdnT, poolT)[b]
                c.e.wait_ge(sems["br_ready"], c.next("br_ready"))
                for k in range(4):
                    c.e.activation(br_hi[:, k, c0:], src[:, k, c0:], ACT.Copy).then_inc(sems["brhi_ready"], 1)

                def trip(last):
                    for j in range(2):
                        act_split(c)
                        bk = tile_wait(c)
                        c.e.wait_ge(sems["merged_ready"], c.next("merged_ready"))
                        c.e.activation(sig[:, j, c0:], ps[:, bk, c0:TOK], ACT.Sigmoid).then_inc(sems["sig_ready"], 1)
                        c.e.drain().then_inc(sems[f"free{bk}"], 1)
                        act_split(c, KD if last and j == 1 else 4)
                        tile_wait(c)

                with c.loop(f"merge{b}{c0}", 3 if b == 2 else 4):
                    trip(False)
                if b == 2:
                    trip(True)
            c.advance("merged_ready", 2)
            c.e.wait_ge(sems["br_ready"], c.next("br_ready"))
            for k in range(KD):
                c.e.activation(h_hi[:, k, c0:], merged[:, k, c0:], ACT.Copy).then_inc(sems["mhi_ready"], 1)
            with c.loop(f"wout{c0}", 2) as it:
                for j in range(4):
                    act_split(c)
                    c.advance("tile")
                    act_square(c, j % 2, bass.ds(it * 4 + j, 1), c0)

        def merge_dve(c, c0, layer, ada_from):
            for b in range(3):
                src = (attnT, gdnT, poolT)[b]
                with_ada = ada_from is not None and b == 0
                for k in range(4):
                    c.e.wait_ge(sems["brhi_ready"], c.next("brhi_ready"))
                    c.e.tensor_tensor(br_lo[:, k, c0:], src[:, k, c0:], br_hi[:, k, c0:].bitcast(F32),
                                      ALU.subtract).then_inc(sems["brlo_ready"], 1)
                if b == 0:
                    for _ in range(2):
                        c.e.drain().then_inc(sems["merged_ready"], 1)

                def trip(it, last):
                    for j in range(2):
                        dve_split(c)
                        c.advance("tile")
                        if with_ada and j == 0:
                            dve_ada_row(c)
                        elif with_ada:
                            dve_ada(c, it * 2 + ada_from)
                        dve_split(c, KD if last and j == 1 else 4)
                        bk = tile_wait(c)
                        c.e.wait_ge(sems["sig_ready"], c.next("sig_ready"))
                        mt = merged[:, bass.ds(it * 2 + j, 1), c0:].rearrange("p a b -> p (a b)")
                        if b == 0:
                            c.e.tensor_tensor(mt, sig[:, j, c0:], ps[:, bk, c0:TOK], ALU.mult) \
                               .then_inc(sems[f"free{bk}"], 1)
                        else:
                            c.e.tensor_tensor(sig[:, j, c0:], sig[:, j, c0:], ps[:, bk, c0:TOK], ALU.mult) \
                               .then_inc(sems[f"free{bk}"], 1)
                            c.e.drain()
                            c.e.tensor_tensor(mt, mt, sig[:, j, c0:], ALU.add)
                        c.e.drain().then_inc(sems["merged_ready"], 1)

                with c.loop(f"merge{b}{with_ada}{c0}", 3 if b == 2 else 4) as it:
                    trip(it, False)
                if b == 2:
                    trip(3, True)
                c.e.drain().then_inc(sems["br_ready"], 1)
            for k in range(KD):
                c.e.wait_ge(sems["mhi_ready"], c.next("mhi_ready"))
                c.e.tensor_tensor(h_lo[:, k, c0:], merged[:, k, c0:], h_hi[:, k, c0:].bitcast(F32),
                                  ALU.subtract).then_inc(sems["mlo_ready"], 1)
            g0 = layer * MOD + 5 * KD
            with_ada = ada_from is not None
            dve_sum_start(c, c0)
            with c.loop(f"wout{with_ada}{c0}", 2) as it:
                for j in range(4):
                    dve_split(c)
                    if with_ada and j == 0:
                        dve_ada_row(c)
                    if with_ada and j == 2:
                        dve_ada(c, it * 2 + ada_from + 8)
                    b = tile_wait(c)
                    for lo, hi, s in sides[c0]:
                        xs = xT[:, bass.ds(it * 4 + j, 1), lo:hi].rearrange("p a b -> p (a b)")
                        gs = mod[:, bass.ds(it * 4 + g0 + j, 1), s:s + 1].rearrange("p a b -> p (a b)")
                        last = c.e.scalar_tensor_tensor(xs, ps[:, b, lo:hi], gs, xs, ALU.mult, ALU.add)
                    last.then_inc(sems[f"free{b}"], 1)
                    dve_sum_square(c, j % 2, c0)

        SETUP = 15

        def setup_sp(c):
            def load(dst, src):
                c.e.dma_start(dst, src).then_inc(sems["dma_setup"], 16)
            load(con[:, :], a["con"])
            load(rows[:, 0:2, :], a["ctx"][0].rearrange("(t p) d -> p t d", p=P))
            load(rows[:, 2:4, :], a["x"][0].rearrange("(t p) d -> p t d", p=P))
            load(vrows[0:KD, 4, :], a["c_ctx"].rearrange("(k p) -> k p", p=P))
            load(vrows[KD:2 * KD, 4, :], a["c"][0].rearrange("(k p) -> k p", p=P))
            for v, name in ((V_N1, "norm_ffn1"), (V_NM, "norm_mix"), (V_N2, "norm_ffn2"), (V_PS, "pool_scale"),
                            (V_GN, "gdn_norm")):
                src = a[name].rearrange("l (k p) -> (l k) p", p=P)
                load(vrows[v:v + src.shape[0], 0, :], src)
            load(vrows[V_FIN:V_END, 0, :], a["final_norm"].rearrange("(k p) -> k p", p=P))
            load(vrows[0:DEPTH * CONV * 12, 1, :], a["gdn_conv"].rearrange("l t (k p) -> (l t k) p", p=P))
            load(vrows[0:MOD, 2:4, :], a["b_ada"].rearrange("l (k p) -> k l p", p=P))
            flat = a["attn_sink"].rearrange("(o l) h -> o (l h)", o=1)
            load(sink[:, :, :].rearrange("p l h -> p (l h)"), flat.to_broadcast([P, DEPTH * HEADS]))
            for t, name in ((alog, "gdn_a_log"), (dtb, "gdn_dt_bias")):
                flat = a[name].rearrange("(o l) d h -> o (l d h)", o=1)
                load(t[:, :, :, :].rearrange("p l d h -> p (l d h)"), flat.to_broadcast([P, DEPTH * 2 * GH]))

        VECS = ((4, 2 * KD), (0, V_END), (1, DEPTH * CONV * 12), (2, MOD), (3, MOD))

        def setup_pe(c):
            for _ in range(CREDIT["tile_done"]):
                c.e.sem_inc(sems["tile_done"], 1)
            c.e.sem_inc(sems["ada_row"], 1)
            c.e.sem_inc(sems["ada_row"], 1)
            c.e.wait_ge(sems["dma_setup"], 16 * (SETUP + 1))
            for i, (slot, n) in enumerate(VECS):
                b = 4 + i % 2
                c.e.wait_ge(sems[f"free{b}"], c.next(f"free{b}"))
                c.e.transpose(ps[:, b, 0:n], vrows[0:n, slot, :], con[0:n, C_ID:C_ID + n]) \
                   .then_inc(sems[f"dve{b}"], 1)
            for k in range(KD):
                b = k % 4
                c.e.wait_ge(sems[f"free{b}"], c.next(f"free{b}"))
                for t in range(4):
                    last = c.e.transpose(ps[:, b, t * P:(t + 1) * P], rows[:, t, k * P:(k + 1) * P], ident)
                last.then_inc(sems[f"dve{b}"], 1)
            c.e.wait_ge(sems["c_ready"], c.next("c_ready"))
            with c.loop("ada", 8):
                pe_ada(c)
                pe_ada_turn(c)

        def setup_dve(c):
            for _ in range(2):
                c.e.sem_inc(sems["sq_used"], 1)
            for b in range(8):
                c.e.sem_inc(sems[f"free{b}"], 1)
            c.e.memset(bias[:, 0:1], EPS)
            c.e.memset(bias[:, 1:2], math.log(GD ** -0.5))
            c.e.memset(bias[:, 2:3], 1.0)
            dst = (cT[:, :, :].rearrange("p s k -> p (s k)"), vec[:, :],
                   convw[:, :, :, :].rearrange("p l t k -> p (l t k)"), bada[:, 0:MOD], bada[:, MOD:2 * MOD])
            for i, (slot, n) in enumerate(VECS):
                b = 4 + i % 2
                c.e.wait_ge(sems[f"dve{b}"], c.next(f"dve{b}"))
                c.e.tensor_copy(dst[i], ps[:, b, 0:n]).then_inc(sems[f"free{b}"], 1)
                if i == 0:
                    c.e.drain().then_inc(sems["zero_ready"], 1)
            for k in range(KD):
                b = k % 4
                c.e.wait_ge(sems[f"dve{b}"], c.next(f"dve{b}"))
                c.e.tensor_copy(xT[:, k, :], ps[:, b, :]).then_inc(sems[f"free{b}"], 1)
            dve_sum_start(c, 0)
            for k in range(KD):
                dve_sum_square(c, k % 2, 0)
            dve_split(c)
            dve_split(c)
            with c.loop("ada", 8) as it:
                dve_ada_row(c)
                dve_ada(c, it * 2)
            c.e.drain()

        def result_dve(c):
            for t in range(KD):
                c.e.tensor_tensor(xT[:, t, LAT:], xT[:, t, LAT:], rstd[:, 0, LAT:], ALU.mult)
                c.e.drain()
                v = V_FIN + t
                c.e.tensor_scalar(xT[:, t, LAT:], xT[:, t, LAT:], vec[:, v:v + 1], None, ALU.mult) \
                   .then_inc(sems["fin_ready"], 1)
            for t in range(2):
                for q in range(2):
                    b = 2 * t + q
                    c.e.wait_ge(sems[f"dve{b}"], c.next(f"dve{b}"))
                    c.e.tensor_copy(rows[:, t, q * 512:(q + 1) * 512], ps[:, b, :])
                c.e.drain().then_inc(sems["o_out"], 1)

        def result_pe(c):
            for _ in range(KD):
                c.e.wait_ge(sems["fin_ready"], c.next("fin_ready"))
            for t in range(2):
                for q in range(2):
                    b = 2 * t + q
                    c.e.wait_ge(sems[f"free{b}"], c.next(f"free{b}"))
                    for k in range(4):
                        last = c.e.transpose(ps[:, b, k * P:(k + 1) * P],
                                             xT[:, 4 * q + k, LAT + t * P:LAT + (t + 1) * P], ident)
                    last.then_inc(sems[f"dve{b}"], 1)

        ADA = {(0, "ffn1"): 16, (0, "qkv"): 50, (0, "late"): 56, (0, "merge"): 60, (0, "ffn2"): 72,
               (1, "ffn1"): 106, (1, "qkv"): None, (1, "late"): 140, (1, "merge"): None, (1, "ffn2"): None}

        block = es.enter_context(nc.Block())

        @block.sync
        def _(eng):
            c = counts(eng, "sp", ())
            setup_sp(c)
            for j in range(2):
                sp_block(c, a["w_ffn1_in"][0], 0, KD, j * P)
                sp_block(c, a["w_ffn1_in"][0], 0, KD, D_FF + j * P)
            with c.loop("ada", 8) as it:
                sp_ada(c, 0, it * 2)
            for layer in range(DEPTH):
                ffn_sp(c, layer, 1, ADA[layer, "ffn1"])
                proj_sp(c, layer, ADA[layer, "qkv"])
                late_sp(c, layer, ADA[layer, "late"])
                merge_sp(c, layer, ADA[layer, "merge"])
                ffn_sp(c, layer, 2, ADA[layer, "ffn2"])
            for t in range(2):
                c.e.wait_ge(sems["o_out"], c.next("o_out"))
                c.e.dma_start(out[0, t * P:(t + 1) * P, :], rows[:, t, :]).then_inc(sems["dma_out"], 16)
            c.e.wait_ge(sems["dma_out"], 32)

        @block.gpsimd
        def _(eng):
            c = counts(eng, "pool", ())
            for layer in range(DEPTH):
                gdn_pool(c)
                c.advance("stage_free", 1)

        @block.tensor
        def _(eng):
            c = counts(eng, "pe", ())
            setup_pe(c)
            for layer in range(DEPTH):
                c0 = 0
                pe_norm(c, 0)
                ffn_pe(c, 0, ADA[layer, "ffn1"])
                c0 = 0 if layer < DEPTH - 1 else LAT
                pe_norm(c, 0)
                proj_pe(c, layer, c0, ADA[layer, "qkv"])
                att_pe(c, c0)
                qk_pe(c)
                gdn_pe(c)
                late_pe(c, c0)
                merge_pe(c, c0, ADA[layer, "merge"])
                pe_norm(c, c0)
                ffn_pe(c, c0, ADA[layer, "ffn2"])
            c.c0 = LAT
            pe_ssq(c)
            result_pe(c)

        @block.scalar
        def _(eng):
            c = counts(eng, "act", ())
            c.e.wait_ge(sems["zero_ready"], c.next("zero_ready"))
            c.e.activation(cT[:, :, :], cT[:, :, :], ACT.Silu).then_inc(sems["c_ready"], 1)
            for k in range(KD):
                act_square(c, k % 2, slice(k, k + 1), 0)
            act_split(c)
            act_split(c)
            for layer in range(DEPTH):
                c.layer = layer
                act_norm(c, 0, layer, 0)
                ffn_act(c, 0, ADA[layer, "ffn1"], False)
                c0 = 0 if layer < DEPTH - 1 else LAT
                act_norm(c, 0, layer, 3)
                proj_act(c, layer, c0, ADA[layer, "qkv"])
                att_act(c, c0, layer)
                qk_act(c)
                gdn_act(c)
                c.advance("stage_free", 1)
                late_act(c, c0)
                merge_act(c, c0, ADA[layer, "merge"])
                act_norm(c, c0, layer, 6)
                ffn_act(c, c0, ADA[layer, "ffn2"], layer == DEPTH - 1)
            act_rstd(c, 4, 0, LAT, 1.0 / D, None)

        @block.vector
        def _(eng):
            c = counts(eng, "dve", ("ada_row",))
            setup_dve(c)
            for layer in range(DEPTH):
                g = layer * KD
                dve_norm(c, 0, V_N1 + g, layer, 1)
                ffn_dve(c, 0, layer, 2, ADA[layer, "ffn1"], False)
                c0 = 0 if layer < DEPTH - 1 else LAT
                dve_norm(c, 0, V_NM + g, layer, 4)
                proj_dve(c, layer, c0, ADA[layer, "qkv"])
                att_dve(c, c0, layer)
                qk_dve(c, layer)
                gdn_dve(c)
                late_dve(c, c0, layer, ADA[layer, "late"])
                merge_dve(c, c0, layer, ADA[layer, "merge"])
                dve_norm(c, c0, V_N2 + g, layer, 7)
                ffn_dve(c, c0, layer, 8, ADA[layer, "ffn2"], layer == DEPTH - 1)
            dve_norm(c, LAT, None, None, None)
            result_dve(c)


def constants():
    i = np.arange(P)
    con = np.zeros((P, C_END), np.float32)

    def put(at, m):
        con[:, at:at + m.shape[1]] = m

    put(C_ID, np.eye(P))
    put(C_ONE, np.ones((P, P)))
    for d in range(2):
        keep = (i[:, None] <= i[None, :]) if d == 0 else (i[:, None] >= i[None, :])
        put(C_TRI + d * P, keep.astype(np.float32))
        put(C_NEG + d * P, np.where(keep, 0.0, NEG))
        for s in range(LEVELS):
            blk = i >> s
            m = ((blk[:, None] % 2 == 0) & (blk[None, :] == blk[:, None] + 1)).astype(np.float32)
            put(C_LEV + (d * LEVELS + s) * P, m if d == 0 else m.T)
    rot = np.zeros((P, P), np.float32)
    half = DH // 4
    for o in range(P):
        if o % (2 * half) < half:
            rot[o + half, o] = -1.0
        else:
            rot[o - half, o] = 1.0
    put(C_ROT, rot)
    for h in range(KV_HEADS):
        dup = np.zeros((P, P), np.float32)
        for o in range(P):
            dup[h * DH + o % DH, o] = 1.0
        put(C_KD + 2 * h * P, dup)
        put(C_KD + (2 * h + 1) * P, dup @ rot)
    inv = (np.float32(10000.0) ** (-np.arange(half, dtype=np.float32) / np.float32(half))).astype(np.float32)
    t = np.arange(SEG)
    for f in range(P):
        pos = (t // 64 if f % DH < DH // 2 else t % 64).astype(np.float32)
        ang = pos * inv[f % half]
        con[f, C_COS:C_COS + SEG] = np.cos(ang)
        con[f, C_SIN:C_SIN + SEG] = np.sin(ang)
    for q in range(2):
        tq = q * P + i
        put(C_MASK + q * TOK + SEG, np.where(np.abs(t[None, :] - tq[:, None]) <= WINDOW, 0.0, NEG))
    for g, w in enumerate(POOL_SIZES):
        cnt = np.clip(t + w // 2, 0, SEG) - np.clip(t - w // 2, 0, SEG)
        r = 1.0 / cnt
        con[:, C_EDGE + 16 * g:C_EDGE + 16 * g + 8] = r[:8]
        con[:, C_EDGE + 16 * g + 8:C_EDGE + 16 * g + 16] = r[-8:]
    return con


_INS = ["x", "c", "ctx", "c_ctx", "w_ada", "b_ada", "norm_ffn1", "w_ffn1_in", "w_ffn1_out", "norm_mix", "w_in",
        "attn_sink", "gdn_conv", "gdn_a_log", "gdn_dt_bias", "gdn_norm", "pool_w", "pool_scale", "w_branch_attn",
        "w_branch_gdn", "w_branch_pool", "w_out", "norm_ffn2", "w_ffn2_in", "w_ffn2_out", "final_norm"]


def kernel(**inputs):
    import concourse.bacc as bacc
    from concourse.bass_utils import run_bass_kernel_spmd as run

    nc = bacc.Bacc("TRN2", target_bir_lowering=False, num_devices=1)
    arrays, args = {}, {}
    for name in _INS + ["con"]:
        v = constants() if name == "con" else np.ascontiguousarray(inputs[name])
        arrays[f"in_{name}"] = v
        args[name] = nc.dram_tensor(f"in_{name}", v.shape, F32, kind="ExternalInput").ap()
    out = nc.dram_tensor("out_0", (1, SEG, D), F32, kind="ExternalOutput").ap()
    learned = {}
    build(nc, args, out, learned)
    if learned:
        raise ValueError("PER_TRIP = " + repr({**PER_TRIP, **learned}))
    r = run(nc, [arrays], core_ids=[0])
    return r.results[0]["out_0"]
```
